# Optimizing a Trainium2 kernel written in Bass

```python
import math
import jax, jax.numpy as jnp
from jax import lax
import numpy as np

D_MODEL = 1024
BATCH = 1
SEQ = 256
DEPTH = 2

HEAD_DIM = 64
N_HEADS_A = 4
DIFF_DIM = HEAD_DIM // 2
N_HEADS_B = 4
N_HEADS_C = 4
N_HEADS_D = 4
BRANCH_WIDTH = 4 * HEAD_DIM
N_BRANCHES = 4
ROPE_THETA = 500000.0
ROPE_FRACTION = 4
Q_BLOCK = 128
DILATED_PATTERNS = ((128, 1), (512, 4), (2048, 16))
D_FF = 2048
CONV_WIDTH = 3
LN_EPS = 1e-5
DEEPNORM_ALPHA = (2.0 * DEPTH) ** 0.25
DEEPNORM_BETA = (8.0 * DEPTH) ** -0.25

kernel_name = 'hybrid_gated_parallel_mixers_deepnorm'

def _layer_norm(x, g, b):
    xf = x.astype(jnp.float32)
    mu = jnp.mean(xf, axis=-1, keepdims=True)
    var = jnp.mean(jnp.square(xf - mu), axis=-1, keepdims=True)
    return ((xf - mu) * lax.rsqrt(var + LN_EPS)).astype(x.dtype) * g + b

def _rms(x):
    xf = x.astype(jnp.float32)
    return (xf * lax.rsqrt(jnp.mean(jnp.square(xf), axis=-1, keepdims=True) + LN_EPS)).astype(x.dtype)

def _heads(t, n):
    b, s, w = t.shape
    return t.reshape(b, s, n, w // n).transpose(0, 2, 1, 3)

def _merge_heads(t):
    b, n, s, d = t.shape
    return t.transpose(0, 2, 1, 3).reshape(b, s, n * d)

def _blocks(t):
    b, h, s, d = t.shape
    return jnp.moveaxis(t.reshape(b, h, s // Q_BLOCK, Q_BLOCK, d), 2, 0)

def _unblocks(t):
    nb, b, h, q, d = t.shape
    return jnp.moveaxis(t, 0, 2).reshape(b, h, nb * q, d)

def _partial_rotary(x, positions):
    dh = x.shape[-1]
    r = dh // ROPE_FRACTION
    half = r // 2
    inv_freq = jnp.power(jnp.float32(ROPE_THETA), -2.0 * jnp.arange(half, dtype=jnp.float32) / r)
    ang = positions.astype(jnp.float32)[:, None, :, None] * inv_freq
    cos, sin = jnp.cos(ang), jnp.sin(ang)
    xr = x[..., :r].astype(jnp.float32)
    x1, x2 = xr[..., :half], xr[..., half:]
    rot = jnp.concatenate([x1 * cos - x2 * sin, x2 * cos + x1 * sin], axis=-1).astype(x.dtype)
    return jnp.concatenate([rot, x[..., r:]], axis=-1)

def _diff_attention(q, k, v, lam):
    b, h2, s, dd = q.shape
    h = h2 // 2
    scale = dd ** -0.5
    kpos = jnp.arange(s)

    def block(args):
        qb, n = args
        sc = jnp.einsum('bhqd,bhkd->bhqk', qb, k).astype(jnp.float32) * scale
        qpos = n * Q_BLOCK + jnp.arange(Q_BLOCK)
        sc = jnp.where(kpos[None, :] <= qpos[:, None], sc, -jnp.inf)
        p = jax.nn.softmax(sc, axis=-1).reshape(b, h, 2, Q_BLOCK, s)
        w = p[:, :, 0] - lam * p[:, :, 1]
        return jnp.einsum('bhqk,bhkd->bhqd', w.astype(v.dtype), v)

    return _unblocks(lax.map(block, (_blocks(q), jnp.arange(s // Q_BLOCK))))

def _stick_breaking_attention(q, k, v):
    b, h, s, d = q.shape
    scale = d ** -0.5
    kpos = jnp.arange(s)

    def block(args):
        qb, n = args
        z = jnp.einsum('bhqd,bhkd->bhqk', qb, k).astype(jnp.float32) * scale
        qpos = n * Q_BLOCK + jnp.arange(Q_BLOCK)
        strict = kpos[None, :] < qpos[:, None]
        log_keep = jnp.where(strict, jax.nn.log_sigmoid(-z), 0.0)
        after = lax.cumsum(log_keep, axis=log_keep.ndim - 1, reverse=True) - log_keep
        a = jnp.where(strict, jnp.exp(jax.nn.log_sigmoid(z) + after), 0.0)
        return jnp.einsum('bhqk,bhkd->bhqd', a.astype(v.dtype), v)

    return _unblocks(lax.map(block, (_blocks(q), jnp.arange(s // Q_BLOCK))))

def _banded_attention(q, k, v, steps):
    *lead, L, d = q.shape
    nb = L // Q_BLOCK
    qb = q.reshape(*lead, nb, Q_BLOCK, d)
    kb = k.reshape(*lead, nb, Q_BLOCK, d)
    vb = v.reshape(*lead, nb, Q_BLOCK, d)
    k_prev = jnp.concatenate([jnp.zeros_like(kb[..., :1, :, :]), kb[..., :-1, :, :]], axis=-3)
    v_prev = jnp.concatenate([jnp.zeros_like(vb[..., :1, :, :]), vb[..., :-1, :, :]], axis=-3)
    kw = jnp.concatenate([k_prev, kb], axis=-2)
    vw = jnp.concatenate([v_prev, vb], axis=-2)
    sc = jnp.einsum('...nqd,...nkd->...nqk', qb, kw).astype(jnp.float32) * (d ** -0.5)
    i = jnp.arange(Q_BLOCK)[:, None]
    j = jnp.arange(2 * Q_BLOCK)[None, :]
    dist = Q_BLOCK + i - j
    blk = jnp.arange(nb)[:, None, None]
    valid = (dist >= 0) & (dist <= steps) & ((blk > 0) | (j >= Q_BLOCK))
    sc = jnp.where(valid, sc, -jnp.inf)
    m = jnp.max(sc, axis=-1, keepdims=True)
    p = jnp.exp(sc - m)
    den = jnp.sum(p, axis=-1, keepdims=True)
    out = jnp.einsum('...nqk,...nkd->...nqd', (p / den).astype(v.dtype), vw)
    lse = (m + jnp.log(den))[..., 0]
    return out.reshape(*lead, L, d), lse.reshape(*lead, L)

def _dilated_attention(q, k, v):
    b, h, s, d = q.shape
    outs, lses = [], []
    for window, dil in DILATED_PATTERNS:
        steps = window // dil
        L = s // dil
        Lp = -(-L // Q_BLOCK) * Q_BLOCK

        def strided(t):
            t = t.reshape(b, h, L, dil, d).transpose(0, 1, 3, 2, 4)
            return jnp.pad(t, ((0, 0), (0, 0), (0, 0), (0, Lp - L), (0, 0)))

        o, lse = _banded_attention(strided(q), strided(k), strided(v), steps)
        outs.append(o[..., :L, :].transpose(0, 1, 3, 2, 4).reshape(b, h, s, d))
        lses.append(lse[..., :L].transpose(0, 1, 3, 2).reshape(b, h, s))
    w = jax.nn.softmax(jnp.stack(lses, axis=0), axis=0)
    return jnp.sum(w[..., None].astype(v.dtype) * jnp.stack(outs, axis=0), axis=0)

def _forgetting_attention(q, k, v, log_f):
    b, h, s, d = q.shape
    scale = d ** -0.5
    F = lax.cumsum(log_f, axis=log_f.ndim - 1)
    kpos = jnp.arange(s)

    def block(args):
        qb, Fq, n = args
        sc = jnp.einsum('bhqd,bhkd->bhqk', qb, k).astype(jnp.float32) * scale
        sc = sc + Fq[..., 0][..., None] - F[:, :, None, :]
        qpos = n * Q_BLOCK + jnp.arange(Q_BLOCK)
        sc = jnp.where(kpos[None, :] <= qpos[:, None], sc, -jnp.inf)
        p = jax.nn.softmax(sc, axis=-1)
        return jnp.einsum('bhqk,bhkd->bhqd', p.astype(v.dtype), v)

    return _unblocks(lax.map(block, (_blocks(q), _blocks(F[..., None]), jnp.arange(s // Q_BLOCK))))

def _mixer_sublayer(h, positions, lambda_init, w_in, lam_q1, lam_k1, lam_q2, lam_k2,
                    subln_g, forget_b, w_branch, w_o):
    b, s, _ = h.shape
    proj = jnp.einsum('bsd,de->bse', h, w_in)
    widths = [BRANCH_WIDTH] * 12 + [N_HEADS_D, N_BRANCHES * D_MODEL]
    cuts = [int(t) for t in np.cumsum(widths)[:-1]]
    (qa, ka, va, qb, kb, vb, qc, kc, vc, qd, kd, vd, f_logit, gate_logit) = jnp.split(proj, cuts, axis=-1)

    lam = jnp.exp(jnp.sum(lam_q1 * lam_k1)) - jnp.exp(jnp.sum(lam_q2 * lam_k2)) + lambda_init
    oa = _diff_attention(_partial_rotary(_heads(qa, 2 * N_HEADS_A), positions),
                         _partial_rotary(_heads(ka, 2 * N_HEADS_A), positions),
                         _heads(va, N_HEADS_A), lam)
    oa = _rms(oa) * subln_g * (1.0 - lambda_init)

    ob = _stick_breaking_attention(_heads(qb, N_HEADS_B), _heads(kb, N_HEADS_B), _heads(vb, N_HEADS_B))

    oc = _dilated_attention(_partial_rotary(_heads(qc, N_HEADS_C), positions),
                            _partial_rotary(_heads(kc, N_HEADS_C), positions),
                            _heads(vc, N_HEADS_C))

    log_f = jax.nn.log_sigmoid((f_logit + forget_b).astype(jnp.float32)).transpose(0, 2, 1)
    od = _forgetting_attention(_heads(qd, N_HEADS_D), _heads(kd, N_HEADS_D), _heads(vd, N_HEADS_D), log_f)

    branches = jnp.stack([_merge_heads(o) for o in (oa, ob, oc, od)], axis=2)
    y = jnp.einsum('bsnc,ncd->bsnd', branches, w_branch)
    gates = jax.nn.sigmoid(gate_logit).reshape(b, s, N_BRANCHES, D_MODEL)
    merged = jnp.sum(gates * y, axis=2)
    return jnp.einsum('bsd,de->bse', merged, w_o)

def _conv_ffn(h, w_up, conv_w, conv_b, w_down):
    u = jnp.einsum('bsd,df->bsf', h, w_up)
    u = lax.conv_general_dilated(u, conv_w[:, None, :], window_strides=(1,),
                                 padding=((CONV_WIDTH - 1, 0),),
                                 dimension_numbers=('NWC', 'WIO', 'NWC'),
                                 feature_group_count=2 * D_FF) + conv_b
    a, g = jnp.split(u, 2, axis=-1)
    return jnp.einsum('bsf,fd->bsd', jax.nn.silu(a) * g, w_down)

def setup_inputs(seed: int = 0) -> dict:
    key = jax.random.key(seed)
    ks = jax.random.split(key, 24)
    f32 = jnp.float32
    n = lambda k, shape: jax.random.normal(k, shape, dtype=f32)
    in_cols = 12 * BRANCH_WIDTH + N_HEADS_D + N_BRANCHES * D_MODEL
    x = n(ks[0], (BATCH, SEQ, D_MODEL))
    c = n(ks[1], (BATCH, D_MODEL))
    positions = (jnp.arange(SEQ, dtype=jnp.int32)[None, :]
                 + jax.random.randint(ks[2], (BATCH, 1), 0, 1024, dtype=jnp.int32))
    return {
        'x': x,
        'c': c,
        'positions': positions,
        'w_ada': n(ks[3], (DEPTH, D_MODEL, 6 * D_MODEL)) * D_MODEL ** -0.5,
        'b_ada': 0.02 * n(ks[4], (DEPTH, 6 * D_MODEL)),
        'w_in': n(ks[5], (DEPTH, D_MODEL, in_cols)) * D_MODEL ** -0.5,
        'lam_q1': 0.1 * n(ks[6], (DEPTH, DIFF_DIM)),
        'lam_k1': 0.1 * n(ks[7], (DEPTH, DIFF_DIM)),
        'lam_q2': 0.1 * n(ks[8], (DEPTH, DIFF_DIM)),
        'lam_k2': 0.1 * n(ks[9], (DEPTH, DIFF_DIM)),
        'subln_g': 1.0 + 0.02 * n(ks[10], (DEPTH, HEAD_DIM)),
        'forget_b': 4.0 + 0.5 * n(ks[11], (DEPTH, N_HEADS_D)),
        'w_branch': n(ks[12], (DEPTH, N_BRANCHES, BRANCH_WIDTH, D_MODEL)) * BRANCH_WIDTH ** -0.5,
        'w_o': n(ks[13], (DEPTH, D_MODEL, D_MODEL)) * D_MODEL ** -0.5 * DEEPNORM_BETA,
        'ln1_g': 1.0 + 0.02 * n(ks[14], (DEPTH, D_MODEL)),
        'ln1_b': 0.02 * n(ks[15], (DEPTH, D_MODEL)),
        'w_up': n(ks[16], (DEPTH, D_MODEL, 2 * D_FF)) * D_MODEL ** -0.5,
        'conv_w': n(ks[17], (DEPTH, CONV_WIDTH, 2 * D_FF)) * CONV_WIDTH ** -0.5,
        'conv_b': 0.02 * n(ks[18], (DEPTH, 2 * D_FF)),
        'w_down': n(ks[19], (DEPTH, D_FF, D_MODEL)) * D_FF ** -0.5 * DEEPNORM_BETA,
        'ln2_g': 1.0 + 0.02 * n(ks[20], (DEPTH, D_MODEL)),
        'ln2_b': 0.02 * n(ks[21], (DEPTH, D_MODEL)),
    }

def reference(x, c, positions, w_ada, b_ada, w_in, lam_q1, lam_k1, lam_q2, lam_k2, subln_g,
              forget_b, w_branch, w_o, ln1_g, ln1_b, w_up, conv_w, conv_b, w_down, ln2_g, ln2_b):
    for l in range(DEPTH):
        lambda_init = 0.8 - 0.6 * math.exp(-0.3 * l)
        mod = jnp.einsum('bd,de->be', jax.nn.silu(c), w_ada[l]) + b_ada[l]
        sh_a, sc_a, g_a, sh_f, sc_f, g_f = [m[:, None, :] for m in jnp.split(mod, 6, axis=-1)]
        h = x * (1.0 + sc_a) + sh_a
        mix = _mixer_sublayer(h, positions, lambda_init, w_in[l], lam_q1[l], lam_k1[l], lam_q2[l],
                              lam_k2[l], subln_g[l], forget_b[l], w_branch[l], w_o[l])
        x = _layer_norm(DEEPNORM_ALPHA * x + g_a * mix, ln1_g[l], ln1_b[l])
        h = x * (1.0 + sc_f) + sh_f
        ffn = _conv_ffn(h, w_up[l], conv_w[l], conv_b[l], w_down[l])
        x = _layer_norm(DEEPNORM_ALPHA * x + g_f * ffn, ln2_g[l], ln2_b[l])
    return x


_drawn_inputs = setup_inputs


def setup_inputs(seed=0):
    import zlib

    import numpy as np

    out = dict(_drawn_inputs(seed))
    spreads = {}
    factors = {'b_ada': 2.748,
     'lam_q1': 8.0,
     'lam_k1': 8.0,
     'lam_q2': 5.157,
     'lam_k2': 8.0,
     'subln_g': 22.23,
     'forget_b': 26.592,
     'conv_b': 7.64}
    for name, (base, spread) in spreads.items():
        noise = np.random.default_rng([zlib.crc32(name.encode()), seed]).standard_normal(out[name].shape)
        drawn = base * np.exp(spread * noise) if base else spread * noise
        out[name] = __import__('jax').numpy.asarray(drawn.astype(out[name].dtype))
    for name, factor in factors.items():
        out[name] = (out[name] * factor).astype(out[name].dtype)
    return out
```

```python
import math
from contextlib import ExitStack

import numpy as np

import concourse.bass as bass
from concourse import mybir

ALU = mybir.AluOpType
ACT = mybir.ActivationFunctionType
AX_X = mybir.AxisListType.X
F32 = mybir.dt.float32
F32R = mybir.dt.float32r
I32 = mybir.dt.int32

P = 128
D = 1024
SEQ = 256
DEPTH = 2
RB = SEQ // P
KT = D // P
DFF = 2048
FT = 2 * DFF // P
HD = 64
BW = 4 * HD
NBR = 4
EPS = 1e-5
ALPHA = (2.0 * DEPTH) ** 0.25
NEG = -1e30
GATE0 = 12 * BW + 4
CA, CC = 4, 8
THETA = 500000.0

RAW = 4
SPLIT = 3
UNITS = 60
U_IN, U_GATE, U_BR, U_O, U_UP, U_DOWN = 0, 12, 28, 32, 36, 52
IN_BLOCKS = [(2 * BW, "RT"), (4 * BW, "TR"), (8 * BW, "RT"), (10 * BW, "TR"), (0, "RR"), (6 * BW, "RR")]
O_ORDER = [(0, 0), (1, 0), (0, 1), (1, 1)]
DOWN_ORDER = [(0, 0), (0, 1), (0, 2), (1, 0), (1, 1), (1, 2), (0, 3), (1, 3)]
ORDER = "BDAC"
HEADS = [(b, h) for b in ORDER for h in range(4)]
ADA_STEPS = [2, 3, 4, 6, 8, 9, 10, 12, 13, 18, 19, 20, 21, 23, 24, 25, 27, 28, 29, 31, 39, 43, 47, 51]
NEXT_CHUNKS = 2
GATE_CHUNKS = (2, 5)
STREAM = []
for _w in range(UNITS):
    STREAM.append(("w", _w))
    if _w - 2 in ADA_STEPS:
        STREAM.append(("ada", ADA_STEPS.index(_w - 2)))
NSTREAM = len(STREAM)
AT = {u: n for n, u in enumerate(STREAM)}
PRE_ADA = 8
assert NSTREAM % RAW == 0 and PRE_ADA % RAW == 0 and UNITS % SPLIT == 0

MM_GROUPS = [(u, 0) for u in range(1, 28, 2)] + [(28 + q, t) for q in range(4) for t in range(2)] \
    + [(34, 0), (35, 0)] + [(u, 0) for u in range(37, 52, 2)] + [(58, 0), (59, 0)]
NMM = len(MM_GROUPS)
MM_AT = {g: n for n, g in enumerate(MM_GROUPS)}
assert NMM % 2 == 0

QK_AFTER = {11: "A", 16: "C"}
OT_AFTER = {14: 0, 18: 1, 22: 2, 25: 3}
ADA_AFTER = {ADA_STEPS[2 * i + 1] + 1: i for i in range(12)}


def score_head(u):
    return u - 5 if 5 <= u < 21 else None


def small_bank_uses():
    uses = [("x", 0, j) for j in range(4)]
    for u in range(UNITS):
        i = score_head(u)
        if i is not None:
            uses += [("s", i, j) for j in range(2 if HEADS[i][0] == "A" else 1)]
        if u in QK_AFTER:
            uses += [("qk", QK_AFTER[u], j) for j in range(2)]
        if u in OT_AFTER:
            uses += [("o", OT_AFTER[u], 0)]
        if u in ADA_AFTER:
            uses += [("ada", ADA_AFTER[u], 0)]
        if u == U_UP - 1:
            uses += [("x", 1, j) for j in range(4)]
    return uses


SMALL = small_bank_uses()
NSMALL = len(SMALL)
S_AT = {k: n for n, k in enumerate(SMALL)}
PRE_SMALL = 6
assert NSMALL % 2 == 0
SCORES = [k for k in SMALL if k[0] == "s"]
K_AT = {k[1:]: n for n, k in enumerate(SCORES)}
NSC = len(SCORES)
PROBS = 5


def prob_slot(i, j):
    return i % 4 if j == 0 else 4


TR = [("cv", 0), ("f", 0)] + [("p", i) for i in range(16)]
NTR = len(TR)

C_IDN = 0
C_STRICT = C_IDN + P
C_CAUSAL = C_STRICT + 3 * P
C_DIL = C_CAUSAL + 3 * P
C_NU = C_DIL + 3 * P
C_FREQ = C_NU + 2 * SEQ
C_LI = C_FREQ + CA + CC
NCONST = C_LI + 2 * DEPTH


def constants():
    t = np.zeros((P, NCONST), np.float32)
    t[:, C_IDN:C_IDN + P] = np.eye(P)
    q = np.arange(P)[:, None]
    for blk, base in ((0, 0), (1, P)):
        k = np.arange(P * (blk + 1))[None, :]
        dist = q + P * blk - k
        put = slice(base, base + P * (blk + 1))
        t[:, C_STRICT:C_STRICT + 3 * P][:, put] = np.where(dist > 0, 0.0, NEG)
        t[:, C_CAUSAL:C_CAUSAL + 3 * P][:, put] = np.where(dist >= 0, 0.0, NEG)
        count = sum(((dist >= 0) & (dist % dil == 0) & (dist <= window)).astype(int)
                    for window, dil in ((128, 1), (512, 4), (2048, 16)))
        t[:, C_DIL:C_DIL + 3 * P][:, put] = np.where(count > 0, np.log(np.maximum(count, 1)), NEG)
    for jt in range(RB):
        j = np.arange(P)[:, None] + P * jt
        t[:, C_NU + SEQ * jt:C_NU + SEQ * (jt + 1)] = np.where(j <= np.arange(SEQ)[None, :], -1.0, 0.0)
    t[:, C_FREQ:C_FREQ + CA] = np.float32(THETA) ** (-2.0 * np.arange(CA, dtype=np.float32) / (2 * CA))
    t[:, C_FREQ + CA:C_FREQ + CA + CC] = np.float32(THETA) ** (-2.0 * np.arange(CC, dtype=np.float32) / (2 * CC))
    for l in range(DEPTH):
        li = 0.8 - 0.6 * math.exp(-0.3 * l)
        t[:, C_LI + l] = li
        t[:, C_LI + DEPTH + l] = 1.0 - li
    return t


ENDS = {u: n for (u, t), n in MM_AT.items()}
PLAIN = [u for u in range(UNITS) if u not in ENDS]
NPLAIN = len(PLAIN)


def unit_end(u):
    if u < 0:
        return True, 0
    return (True, ENDS[u] + 1) if u in ENDS else (False, PLAIN.index(u) + 1)


ONE = 1


class Own:

    def __init__(self, eng, sem, per_layer):
        self.eng, self.sem, self.per_layer = eng, sem, per_layer
        self.before, self.n, self.layer = 0, 0, 0

    def mark(self, ins):
        ins.then_inc(self.sem, 1)
        self.n += 1
        return self.n

    def after(self, n):
        self.eng.wait_ge(self.sem, self.layer * self.per_layer + (self.before + n))

    def link(self, ins):
        self.after(self.mark(ins))

    def enter(self, layer):
        self.before, self.n, self.layer = self.n, 0, layer

    def leave(self):
        assert self.n == self.per_layer, (self.sem, self.n)


ACT_OWN, DVE_OWN = 24, 216


def build(nc, x, c, positions, w_ada, b_ada, w_in, lam_q1, lam_k1, lam_q2, lam_k2, subln_g, forget_b, w_branch, w_o,
          ln1_g, ln1_b, w_up, conv_w, conv_b, w_down, ln2_g, ln2_b, table, out):
    with ExitStack() as ctx:
        def sb(name, shape, dt=F32):
            return ctx.enter_context(nc.sbuf_tensor(name, shape, dt))

        def sem(name):
            return ctx.enter_context(nc.semaphore(name))

        raw = sb("raw", [P, RAW, 2048])
        w_hi = sb("w_hi", [P, SPLIT, 2048], F32R)
        w_lo = sb("w_lo", [P, SPLIT, 2048], F32R)
        xr = sb("xr", [P, RB, D])
        h_hi = sb("h_hi", [P, KT, SEQ], F32R)
        h_lo = sb("h_lo", [P, KT, SEQ], F32R)
        br_hi = sb("br_hi", [P, KT, SEQ], F32R)
        br_lo = sb("br_lo", [P, KT, SEQ], F32R)
        with ExitStack() as phase:
            gates = phase.enter_context(nc.sbuf_tensor("gates", [P, 4, 8, SEQ], F32))
        with ExitStack() as phase:
            def early(name, shape):
                return phase.enter_context(nc.sbuf_tensor(name, shape, F32))
            early("gates_first_half", [P, 4096])
            q_T = [early(f"q_T{i}", [P, 2, SEQ]) for i in range(2)]
            k_T = [early(f"k_T{i}", [P, 2, SEQ]) for i in range(2)]
            qk_rows = early("qk_rows", [P, RB, 2, BW])
            v_b = early("v_b", [P, RB, BW])
            v_d = early("v_d", [P, RB, BW])
        act_hi = sb("act_hi", [P, 16, SEQ], F32R)
        act_lo = sb("act_lo", [P, 16, SEQ], F32R)
        v_a = sb("v_a", [P, RB, BW])
        v_c = sb("v_c", [P, RB, BW])
        v_of = {"A": v_a, "B": v_b, "C": v_c, "D": v_d}
        with ExitStack() as phase:
            h_f32 = phase.enter_context(nc.sbuf_tensor("h_f32", [P, KT, SEQ], F32))
        with ExitStack() as phase:
            c_rows = phase.enter_context(nc.sbuf_tensor("c_rows", [8, P], F32))
            b_rows = phase.enter_context(nc.sbuf_tensor("b_rows", [96, P], F32))
            lam_in = phase.enter_context(nc.sbuf_tensor("lam_in", [P, 4, DEPTH, 32], F32))
            ang_k = phase.enter_context(nc.sbuf_tensor("ang_k", [P, RB, CA + CC], F32))
        with ExitStack() as phase:
            y_a = phase.enter_context(nc.sbuf_tensor("y_a", [P, 4, SEQ], F32))
            y_g = phase.enter_context(nc.sbuf_tensor("y_g", [P, 4, SEQ], F32))
            th = phase.enter_context(nc.sbuf_tensor("th", [P, 4, SEQ], F32))
        with ExitStack() as phase:
            gated = phase.enter_context(nc.sbuf_tensor("gated", [P, 2, 4, SEQ], F32))
        probs = sb("probs", [P, PROBS, 384])
        with ExitStack() as phase:
            o_sq = phase.enter_context(nc.sbuf_tensor("o_sq", [P, RB, 4, HD], F32))
        soft = sb("soft", [P, 2, 384])
        p_T = sb("p_T", [P, 2, 384])
        o_rows = sb("o_rows", [P, RB, 4, HD])
        lf_b = sb("lf_b", [P, 8, P])
        acc = sb("acc", [P, 2, 512])
        g_row = sb("g_row", [P, D])
        ln_g = sb("ln_g", [P, D])
        ln_b = sb("ln_b", [P, D])
        tab = sb("tab", [P, NCONST])
        ones = sb("ones", [P, SEQ])
        sc_col = sb("sc_col", [P, KT])
        sc_tmp = sb("sc_tmp", [P, 2, KT])
        b_col = sb("b_col", [P, 96])
        mod = sb("mod", [P, 4, KT])
        cv_rows = sb("cv_rows", [P, P])
        cv = sb("cv", [P, P])
        wf = sb("wf", [P, DEPTH * KT, 4])
        wf_hi = sb("wf_hi", [P, KT, 4], F32R)
        wf_lo = sb("wf_lo", [P, KT, 4], F32R)
        f_b = sb("f_b", [P, DEPTH, 4])
        f_v = sb("f_v", [P, RB, 4])
        f_l = sb("f_l", [P, RB, 4])
        f_lf = sb("f_lf", [P, RB, 4])
        pos_i = sb("pos_i", [P, RB], I32)
        pos_f = sb("pos_f", [P, RB])
        ang = sb("ang", [P, RB, CA + CC])
        ang_c = sb("ang_c", [P, RB, CA + CC])
        sin_t = sb("sin_t", [P, RB, CA + CC])
        cos_t = sb("cos_t", [P, RB, CA + CC])
        rot = sb("rot", [P, 4, 128])
        lam_s = sb("lam_s", [P, 2, DEPTH])
        lam_n = sb("lam_n", [P, DEPTH])
        sub_g = sb("sub_g", [P, DEPTH, HD])
        lam_cur = sb("lam_cur", [P, 1])
        sub_cur = sb("sub_cur", [P, HD])
        fb_cur = sb("fb_cur", [P, 4])
        nmax = sb("nmax", [P, NSC, 2])
        tmax = sb("tmax", [P, NSC, 2])
        den = sb("den", [P, NSC, 2])
        rden = sb("rden", [P, 4, RB, 4])
        rsub = sb("rsub", [P, 4, 2, 2])
        stats = sb("stats", [P, RB, 2, 6])
        mv = sb("mv", [P, RB, 2])
        ve = sb("ve", [P, 8])
        rstd = sb("rstd", [P, 8])
        nhalf = sb("nhalf", [P, 8])

        def psum(name):
            return ctx.enter_context(nc.psum_tensor(name, [P, 512], F32))

        mm = [ctx.enter_context(nc.psum_tensor(f"mm{i}", [P, 4, SEQ], F32)) for i in range(2)]
        small = [psum("small0"), psum("small1")]
        turn = psum("turn")
        ov = psum("ov")
        idn = tab[:, C_IDN:C_IDN + P]

        raw_in = [sem(f"raw_in{i}") for i in range(RAW)]
        hi_ready, lo_ready = sem("hi_ready"), sem("lo_ready")
        unit_done = sem("unit_done")
        mm_full = sem("mm_full")
        mm_free = [sem("mm_free0"), sem("mm_free1")]
        s_full = sem("s_full")
        s_free = [sem("s_free0"), sem("s_free1")]
        tr_full, tr_free = sem("tr_full"), sem("tr_free")
        ov_full, ov_free = sem("ov_full"), sem("ov_free")
        small_in, x_in = sem("small_in"), sem("x_in")
        cv_in, g_in, ln_in = sem("cv_in"), sem("g_in"), sem("ln_in")
        h_hi_ready, h_lo_ready = sem("h_hi_ready"), sem("h_lo_ready")
        rope_ready = sem("rope_ready")
        f_ready, lf_ready, wf_ready = sem("f_ready"), sem("lf_ready"), sem("wf_ready")
        z_ready, log_ready, la_ready = sem("z_ready"), sem("log_ready"), sem("la_ready")
        sm_ready, exp_ready = sem("sm_ready"), sem("exp_ready")
        mix_ready = sem("mix_ready")
        pt_ready, pv_done = sem("pt_ready"), sem("pv_done")
        o_ready = sem("o_ready")
        br_hi_ready, br_lo_ready = sem("br_hi_ready"), sem("br_lo_ready")
        gate_ready, merged_ready = sem("gate_ready"), sem("merged_ready")
        m_hi_ready, m_lo_ready = sem("m_hi_ready"), sem("m_lo_ready")
        half_ready, acc_ready, mod_ready = sem("half_ready"), sem("acc_ready"), sem("mod_ready")
        cv_ready, base_ready, conv_ready = sem("cv_ready"), sem("base_ready"), sem("conv_ready")
        tanh_ready, prod_ready = sem("tanh_ready"), sem("prod_ready")
        act_hi_ready, act_lo_ready = sem("act_hi_ready"), sem("act_lo_ready")
        var_ready, rstd_ready = sem("var_ready"), sem("rstd_ready")
        x_done = sem("x_done")
        pre_act, pre_dve, pre_pe = sem("pre_act"), sem("pre_dve"), sem("pre_pe")
        act_own, dve_own = sem("act_own"), sem("dve_own")
        seen_sp, seen_dve = sem("seen_sp"), sem("seen_dve")
        nhalf_ready, out_done = sem("nhalf_ready"), sem("out_done")

        def ktiles(w):
            return w.rearrange("l (k p) n -> p (l k) n", p=P)
        ada_v, in_v, o_v, up_v, down_v = (ktiles(w) for w in (w_ada, w_in, w_o, w_up, w_down))
        br_v = w_branch.rearrange("l n (k p) d -> p (l n k) d", p=P)

        def wide(slot):
            return raw[:, slot, :].rearrange("p (k n) -> p k n", k=4)

        block = ctx.enter_context(nc.Block())

        @block.sync
        def _(sp):
            def slot_free(n, layer):
                if n < RAW:
                    sp.wait_ge(acc_ready, 2 + n // 2 + 1) if n % 2 else sp.wait_ge(half_ready, 2 + n // 2 + 1)
                    sp.wait_ge(lo_ready, layer * UNITS + ONE)
                    return
                kind, w = STREAM[n - RAW]
                if kind == "w":
                    sp.wait_ge(lo_ready, layer * UNITS + (ONE + w + 1))
                else:
                    sp.wait_ge(acc_ready if w % 2 else half_ready, layer * 12 + (4 + w // 2 + 1))

            sp.dma_start(tab[:, :], table).then_inc(small_in, 16)
            sp.dma_start(c_rows[:, :], c.rearrange("b (k p) -> (b k) p", p=P)).then_inc(small_in, 16)
            sp.dma_start(b_rows[:, :], b_ada.rearrange("l (k p) -> (l k) p", p=P)).then_inc(small_in, 16)
            for a in range(PRE_ADA):
                if a >= RAW:
                    sp.wait_ge(acc_ready if a % 2 else half_ready, (a - RAW) // 2 + 1)
                sp.dma_start(wide(a % RAW), ada_v[:, 4 * (a % 2):4 * (a % 2) + 4,
                                                  512 * (a // 2):512 * (a // 2) + 512]).then_inc(raw_in[a % RAW], 16)
            with sp.Fori(0, DEPTH) as l:
                k_d = [sp.snap(l * KT + 4 * i) for i in range(2)]
                k_f = [sp.snap(l * 2 * KT + 4 * i) for i in range(4)]
                for n, (kind, w) in enumerate(STREAM):
                    slot = n % RAW
                    dst = wide(slot)
                    if kind == "ada":
                        chunk, half = w // 4, w % 4
                        col = D * chunk + 512 * (half // 2)
                        k0 = (DEPTH - 1) * KT + 4 * (half % 2)
                        src = ada_v[:, k0:k0 + 4, col:col + 512] if chunk < NEXT_CHUNKS \
                            else ada_v[:, bass.ds(k_d[half % 2], 4), col:col + 512]
                    elif w < U_GATE:
                        col = IN_BLOCKS[w // 2][0]
                        src = in_v[:, bass.ds(k_d[w % 2], 4), col:col + 512]
                    elif w < U_BR:
                        col = GATE0 + 512 * ((w - U_GATE) // 2)
                        src = in_v[:, bass.ds(k_d[w % 2], 4), col:col + 512]
                    elif w < U_O:
                        dst = raw[:, slot, :].rearrange("p (k n) -> p k n", k=8)
                        src = br_v[:, bass.ds(k_d[0], 8), 256 * (w - U_BR):256 * (w - U_BR) + 256]
                    elif w < U_UP:
                        ob, kb = O_ORDER[w - U_O]
                        src = o_v[:, bass.ds(k_d[kb], 4), 512 * ob:512 * ob + 512]
                    elif w < U_DOWN:
                        m = (w - U_UP) // 2
                        col = DFF * (m % 2) + 512 * (m // 2)
                        src = up_v[:, bass.ds(k_d[w % 2], 4), col:col + 512]
                    else:
                        ob, kb = DOWN_ORDER[w - U_DOWN]
                        src = down_v[:, bass.ds(k_f[kb], 4), 512 * ob:512 * ob + 512]
                    slot_free(n, l)
                    sp.sem_inc(seen_sp, 1)
                    sp.dma_start(dst, src).then_inc(raw_in[slot], 16)
            sp.wait_ge(x_done, ONE + 2 * DEPTH)
            sp.dma_start(out.rearrange("b (r p) d -> p (b r) d", p=P), xr[:, :, :]).then_inc(out_done, 16)
            sp.wait_ge(out_done, 16)

        @block.gpsimd
        def _(pool):
            pool.memset(nhalf[:, :], -0.5).then_inc(nhalf_ready, 1)
            pool.dma_start(xr[:, :, :], x.rearrange("b (r p) d -> p (b r) d", p=P)).then_inc(x_in, 16)
            pool.dma_start(pos_i[:, :], positions.rearrange("b (r p) -> p (b r)", p=P),
                           allow_slow_non_contiguous=True).then_inc(x_in, 16)
            for i, v in enumerate((lam_q1, lam_k1, lam_q2, lam_k2)):
                pool.dma_start(lam_in[:, i, :, :], v.partition_broadcast(P)).then_inc(x_in, 16)
            pool.dma_start(sub_g[:, :, :], subln_g.partition_broadcast(P)).then_inc(x_in, 16)
            pool.dma_start(f_b[:, :, :], forget_b.partition_broadcast(P)).then_inc(x_in, 16)
            pool.dma_start(wf[:, :, :], in_v[:, :, 12 * BW:12 * BW + 4]).then_inc(x_in, 16)
            pool.wait_ge(nhalf_ready, 1)

            def power(layer, k, n):
                pool.wait_ge(var_ready, layer * 3 + (k + 1))
                pool.tensor_tensor(rstd[:, 0:n], ve[:, 0:n], nhalf[:, 0:n], ALU.pow).then_inc(rstd_ready, 1)

            def row(t, layer, lo, n):
                return t[bass.ds(layer, 1), lo:lo + n].rearrange("l n -> (l n)").partition_broadcast(P)

            with pool.Fori(0, DEPTH) as l:
                pool.wait_ge(x_done, l * 2 + ONE)
                pool.dma_start(cv_rows[0:96, :], conv_w.rearrange("l t (k p) -> (l t k) p", p=P)[
                    bass.ds(l * 96, 96), :]).then_inc(cv_in, 16)
                pool.dma_start(cv_rows[96:128, :], conv_b.rearrange("l (k p) -> (l k) p", p=P)[
                    bass.ds(l * 32, 32), :]).then_inc(cv_in, 16)
                pool.dma_start(g_row[:, :], row(b_ada, l, 2 * D, D)).then_inc(g_in, 16)
                pool.dma_start(ln_g[:, :], row(ln1_g, l, 0, D)).then_inc(ln_in, 16)
                pool.dma_start(ln_b[:, :], row(ln1_b, l, 0, D)).then_inc(ln_in, 16)
                power(l, 0, 8)
                power(l, 1, 2)
                pool.wait_ge(x_done, l * 2 + (ONE + 1))
                pool.dma_start(g_row[:, :], row(b_ada, l, 5 * D, D)).then_inc(g_in, 16)
                pool.dma_start(ln_g[:, :], row(ln2_g, l, 0, D)).then_inc(ln_in, 16)
                pool.dma_start(ln_b[:, :], row(ln2_b, l, 0, D)).then_inc(ln_in, 16)
                power(l, 2, 2)

        @block.scalar
        def _(act):
            own = Own(act, act_own, ACT_OWN)
            act.sem_inc(pt_ready, ONE)

            act.wait_ge(s_full, 1)
            act.activation(sc_tmp[:, 0, :], small[0][:, 0:KT], ACT.Copy).then_inc(pre_act, 1)
            act.activation(sc_tmp[:, 1, :], small[0][:, 0:KT], ACT.Tanh, scale=0.5).then_inc(s_free[0], 1)
            act.wait_ge(s_full, 2)
            act.activation(b_col[:, :], small[1][:, 0:96], ACT.Copy).then_inc(s_free[1], 1)
            act.wait_ge(pre_dve, 1)
            act.activation(lam_s[:, :, :], lam_s[:, :, :], ACT.Exp).then_inc(pre_act, 1)
            act.wait_ge(pre_dve, 2)
            act.activation(sin_t[:, :, :], ang[:, :, :], ACT.Sin).then_inc(pre_act, 1)
            act.activation(cos_t[:, :, :], ang_c[:, :, :], ACT.Sin).then_inc(pre_act, 1)

            with act.Fori(0, DEPTH) as l:
                own.enter(l)

                def hi(w):
                    n = AT[("w", w)]
                    s, g = n % RAW, (PRE_ADA + n) // RAW + 1
                    act.wait_ge(raw_in[s], l * (16 * NSTREAM // RAW) + 16 * g)
                    kind, n_done = unit_end(w - SPLIT)
                    act.wait_ge(mm_full if kind else unit_done, l * (NMM if kind else NPLAIN) + (ONE + n_done))
                    act.activation(w_hi[:, w % SPLIT, :], raw[:, s, :], ACT.Copy).then_inc(hi_ready, 1)

                def modulate(which):
                    act.wait_ge(mod_ready, l * 8 + (4 if which == 0 else 12))
                    for j in range(4):
                        k = S_AT[("x", which, j)]
                        act.wait_ge(s_full, l * NSMALL + (PRE_SMALL + k + 1))
                        for t in range(2):
                            ft = 2 * j + t
                            last = act.activation(h_f32[:, ft, :], small[k % 2][:, SEQ * t:SEQ * t + SEQ], ACT.Identity,
                                                  bias=mod[:, 2 * which, ft:ft + 1],
                                                  scale=mod[:, 2 * which + 1, ft:ft + 1])
                            if t == 0:
                                own.mark(last)
                        last.then_inc(s_free[k % 2], 1)
                        own.after(own.n)
                        act.wait_ge(s_free[k % 2], l * (NSMALL // 2) + (PRE_SMALL // 2 + k // 2 + 2))
                        act.activation(h_hi[:, 2 * j:2 * j + 2, :], h_f32[:, 2 * j:2 * j + 2, :],
                                       ACT.Copy).then_inc(h_hi_ready, 1)

                def mm_wait(u, t=0):
                    n = MM_AT[(u, t)]
                    act.wait_ge(mm_full, l * NMM + (ONE + n + 1))
                    return mm[n % 2], mm_free[n % 2]

                def projections(b):
                    bank, free = mm_wait(2 * b + 1)
                    if b == 5:
                        act.wait_ge(s_full, l * NSMALL + (PRE_SMALL + S_AT[("qk", "A", 1)] + 1))
                    where = [(v_a, q_T[0]), (k_T[0], v_b), (v_c, q_T[1]), (k_T[1], v_d)]
                    for half in range(2):
                        src = bank[:, 2 * half:2 * half + 2, :]
                        if b < 4:
                            dst = where[b][half]
                            scale = 0.125 if dst in (q_T[0], q_T[1]) else 1.0
                            ins = act.activation(dst[:, :, :], src, ACT.Copy, scale=scale)
                        else:
                            ins = act.activation(qk_rows[:, :, half, :], src, ACT.Copy)
                        own.mark(ins) if half == 0 else ins.then_inc(free, 1)

                def gate(g):
                    bank, free = mm_wait(U_GATE + 2 * g + 1)
                    act.activation(gates[:, g // 2, 4 * (g % 2):4 * (g % 2) + 4, :], bank[:, :, :], ACT.Tanh,
                                   scale=0.5).then_inc(free, 1)

                def softplus_log(src, dst):
                    own.link(act.activation(dst, src, ACT.Abs))
                    own.link(act.activation(dst, dst, ACT.Exp, scale=-1.0))
                    act.activation(dst, dst, ACT.Ln, bias=1.0).then_inc(log_ready, 1)

                def head_first(i):
                    b, h = HEADS[i]
                    if b == "B":
                        act.wait_ge(z_ready, l * 4 + (h + 1))
                        k = K_AT[(i, 0)]
                        softplus_log(probs[:, prob_slot(i, 0), :], soft[:, h % 2, :])
                        return
                    for j in range(2 if b == "A" else 1):
                        k = K_AT[(i, j)]
                        act.wait_ge(sm_ready, l * 16 + (k - 4 + 1))
                        pr = probs[:, prob_slot(i, j), :]
                        act.activation(pr[:, 0:P], pr[:, 0:P], ACT.Exp, bias=nmax[:, k, 0:1],
                                       accum_out=den[:, k, 0:1]).then_inc(exp_ready, 1)
                        act.activation(pr[:, P:3 * P], pr[:, P:3 * P], ACT.Exp, bias=nmax[:, k, 1:2],
                                       accum_out=den[:, k, 1:2]).then_inc(exp_ready, 1)

                def head_second(i):
                    b, h = HEADS[i]
                    if b == "B":
                        act.wait_ge(la_ready, l * 4 + (h + 1))
                        pr = probs[:, prob_slot(i, 0), :]
                        act.activation(pr, pr, ACT.Exp).then_inc(exp_ready, 1)

                def probs_T(i):
                    act.wait_ge(tr_full, l * NTR + (TR.index(("p", i)) + 1))
                    if i >= 2:
                        act.wait_ge(pv_done, l * 16 + (i - 1))
                    act.activation(p_T[:, i % 2, :], turn[:, 0:384], ACT.Copy).then_inc(pt_ready, 1)

                def qk_T(b):
                    s = 0 if b == "A" else 1
                    for j in range(2):
                        k = S_AT[("qk", b, j)]
                        act.wait_ge(s_full, l * NSMALL + (PRE_SMALL + k + 1))
                        dst = (q_T if j == 0 else k_T)[s]
                        act.activation(dst[:, :, :], small[k % 2][:, :].rearrange("p (t q) -> p t q", t=2), ACT.Copy,
                                       scale=0.125 if (b, j) == ("C", 0) else 1.0).then_inc(s_free[k % 2], 1)

                def branch_hi(o):
                    k = S_AT[("o", o, 0)]
                    n = "ABCD".index(ORDER[o])
                    act.wait_ge(s_full, l * NSMALL + (PRE_SMALL + k + 1))
                    act.activation(br_hi[:, 2 * n:2 * n + 2, :], small[k % 2][:, :].rearrange("p (t q) -> p t q", t=2),
                                   ACT.Copy).then_inc(br_hi_ready, 1)

                def merged_hi(dt):
                    act.wait_ge(merged_ready, l * KT + (dt + 1))
                    act.activation(h_hi[:, dt, :], gated[:, dt % 2, 0, :], ACT.Copy, scale=0.5).then_inc(m_hi_ready, 1)

                def conv_base(m):
                    bank, _ = mm_wait(U_UP + 2 * m + 1)
                    if m >= 2:
                        act.wait_ge(act_lo_ready, l * 4 + m // 2)
                    y = (y_a, y_g)[m % 2]
                    for t in range(4):
                        f = 16 * (m % 2) + 4 * (m // 2) + t
                        act.activation(y[:, t, :], bank[:, t, :], ACT.Identity, bias=cv[:, 96 + f:97 + f],
                                       scale=cv[:, 64 + f:65 + f]).then_inc(base_ready, 1)

                def ffn_tanh(j):
                    act.wait_ge(conv_ready, l * 4 + (j + 1))
                    act.activation(th[:, :, :], y_a[:, :, :], ACT.Tanh, scale=0.5).then_inc(tanh_ready, 1)

                def ffn_hi(j):
                    act.wait_ge(prod_ready, l * 4 + (j + 1))
                    act.activation(act_hi[:, 4 * j:4 * j + 4, :], y_g[:, :, :], ACT.Copy).then_inc(act_hi_ready, 1)

                hi(0)
                hi(1)
                hi(2)
                modulate(0)
                hi(3)
                act.wait_ge(tr_full, l * NTR + 1)
                act.activation(cv[:, :], turn[:, 0:P], ACT.Copy).then_inc(tr_free, 1)

                for s in range(2, UNITS + 1):
                    if U_UP + 3 <= s <= U_DOWN + 1 and s % 2:
                        m = (s - U_UP - 3) // 2
                        (ffn_hi if m % 2 else ffn_tanh)(m // 2)
                    if s + 2 < UNITS:
                        hi(s + 2)
                    if s - 1 in QK_AFTER:
                        qk_T(QK_AFTER[s - 1])
                    if s % 2 == 0 and s <= 12:
                        projections(s // 2 - 1)
                    if s == 2:
                        act.wait_ge(f_ready, l + 1)
                        softplus_log(f_v[:, :, :], f_l[:, :, :])
                    if s % 2 == 0 and 14 <= s <= 28:
                        gate(s // 2 - 7)
                    if 0 <= s - 9 < 16:
                        probs_T(s - 9)
                    if 0 <= s - 7 < 16:
                        head_second(s - 7)
                    if 0 <= s - 6 < 16:
                        head_first(s - 6)
                    if s - 1 in OT_AFTER:
                        branch_hi(OT_AFTER[s - 1])
                    if U_BR < s <= U_BR + 4:
                        merged_hi(2 * (s - U_BR - 1))
                        merged_hi(2 * (s - U_BR - 1) + 1)
                    if s == U_UP:
                        modulate(1)
                    if U_UP + 2 <= s <= U_DOWN and s % 2 == 0:
                        m = (s - U_UP) // 2 - 1
                        conv_base(m)
                own.leave()

        @block.vector
        def _(dve):
            own = Own(dve, dve_own, DVE_OWN)
            dve.sem_inc(lo_ready, ONE)
            own.link(dve.memset(ones[:, :], 1.0))

            def ada_unit(slot, half, buf):
                for k in range(4):
                    wk = wide(slot)[:, k, :]
                    sc = sc_col[:, 4 * half + k:4 * half + k + 1]
                    if half == 0 and k == 0:
                        ins = dve.tensor_scalar(acc[:, buf, :], wk, sc, None, ALU.mult)
                    else:
                        ins = dve.scalar_tensor_tensor(out=acc[:, buf, :], in0=wk, scalar=sc, in1=acc[:, buf, :],
                                                       op0=ALU.mult, op1=ALU.add)
                    if k < 3:
                        own.link(ins)
                    else:
                        ins.then_inc(acc_ready if half else half_ready, 1)

            def column(k, row, half, bias):
                src = small[k % 2][:, 0:4]
                dst = mod[:, row, 4 * half:4 * half + 4]
                if row % 2:
                    return dve.scalar_tensor_tensor(out=dst, in0=src, scalar=1.0, in1=bias, op0=ALU.add, op1=ALU.add)
                return dve.tensor_tensor(dst, src, bias, ALU.add)

            dve.wait_ge(pre_act, 1)
            dve.wait_ge(s_free[0], 2)
            own.link(dve.tensor_scalar(sc_tmp[:, 1, :], sc_tmp[:, 1, :], 0.5, 0.5, ALU.mult, ALU.add))
            own.link(dve.tensor_tensor(sc_col[:, :], sc_tmp[:, 0, :], sc_tmp[:, 1, :], ALU.mult))
            for a in range(PRE_ADA):
                dve.wait_ge(raw_in[a % RAW], 16 * (a // RAW + 1))
                if a % 2 == 0 and a >= 4:
                    dve.wait_ge(s_full, 2 + a // 2 - 1)
                if a % 2:
                    dve.wait_ge(half_ready, a // 2 + 1)
                ada_unit(a % RAW, a % 2, (a // 2) % 2)
            dve.wait_ge(x_in, 16 * 9)
            dve.wait_ge(small_in, 48)
            for i in range(2):
                own.link(dve.tensor_tensor(lam_in[:, 2 * i, :, :], lam_in[:, 2 * i, :, :], lam_in[:, 2 * i + 1, :, :],
                                           ALU.mult))
                ins = dve.tensor_reduce(lam_s[:, i, :], lam_in[:, 2 * i, :, :], AX_X, ALU.add)
                own.link(ins)
            dve.sem_inc(pre_dve, 1)
            own.link(dve.tensor_copy(pos_f[:, :], pos_i[:, :]))
            for r in range(RB):
                ins = dve.tensor_scalar(ang[:, r, :], tab[:, C_FREQ:C_FREQ + CA + CC], pos_f[:, r:r + 1], None, ALU.mult)
            own.link(ins)
            big = 1.5 * 2.0 ** 23
            own.link(dve.tensor_scalar(ang_k[:, :, :], ang[:, :, :], 1.0 / (2.0 * math.pi), big, ALU.mult, ALU.add))
            own.link(dve.tensor_scalar(ang_k[:, :, :], ang_k[:, :, :], big, None, ALU.subtract))
            rest = 2.0 * math.pi
            for bits in (5, 13, 21, 60):
                part = rest if bits == 60 else math.floor(rest * 2.0 ** bits) / 2.0 ** bits
                rest -= part
                own.link(dve.scalar_tensor_tensor(out=ang[:, :, :], in0=ang_k[:, :, :], scalar=-part, in1=ang[:, :, :],
                                                  op0=ALU.mult, op1=ALU.add))
            pi = 3.1415925
            own.link(dve.tensor_scalar(ang[:, :, :], ang[:, :, :], pi, -pi, ALU.min, ALU.max))
            own.link(dve.tensor_scalar(ang_c[:, :, :], ang[:, :, :], math.pi / 2, None, ALU.add))
            own.link(dve.tensor_scalar(ang_k[:, :, :], ang_c[:, :, :], math.pi, -2.0 * math.pi, ALU.is_gt, ALU.mult))
            own.link(dve.tensor_tensor(ang_c[:, :, :], ang_c[:, :, :], ang_k[:, :, :], ALU.add))
            dve.tensor_scalar(ang_c[:, :, :], ang_c[:, :, :], pi, -pi, ALU.min, ALU.max).then_inc(pre_dve, 1)
            dve.wait_ge(pre_act, 2)
            own.link(dve.tensor_tensor(lam_n[:, :], lam_s[:, 1, :], lam_s[:, 0, :], ALU.subtract))
            own.link(dve.tensor_tensor(lam_n[:, :], lam_n[:, :], tab[:, C_LI:C_LI + DEPTH], ALU.subtract))
            for l0 in range(DEPTH):
                own.link(dve.tensor_scalar(sub_g[:, l0, :], sub_g[:, l0, :], tab[:, C_LI + DEPTH + l0:C_LI + DEPTH + l0 + 1],
                                           None, ALU.mult))
            dve.wait_ge(s_free[1], 2)
            for k in range(4):
                dve.wait_ge(s_full, 2 + k + 1)
                column(k, k // 2, k % 2, b_col[:, 4 * k:4 * k + 4]).then_inc(s_free[k % 2], 1)
            dve.wait_ge(s_free[0], 4)
            dve.wait_ge(s_free[1], 4)
            dve.sem_inc(mod_ready, 4)
            dve.sem_inc(x_done, ONE)
            dve.wait_ge(pre_act, 4)

            with dve.Fori(0, DEPTH) as l:
                own.enter(l)

                def lo(w):
                    n = AT[("w", w)]
                    dve.wait_ge(hi_ready, l * UNITS + (w + 1))
                    dve.tensor_tensor(w_lo[:, w % SPLIT, :], raw[:, n % RAW, :], w_hi[:, w % SPLIT, :].bitcast(F32),
                                      ALU.subtract).then_inc(lo_ready, 1)

                def ada(a):
                    n = AT[("ada", a)]
                    blk = a // 2
                    dve.wait_ge(raw_in[n % RAW], l * (16 * NSTREAM // RAW) + 16 * ((PRE_ADA + n) // RAW + 1))
                    if a % 2 == 0 and blk >= 2:
                        dve.wait_ge(s_full, l * NSMALL + (PRE_SMALL + S_AT[("ada", blk - 2, 0)] + 1))
                    if a % 2:
                        dve.wait_ge(half_ready, l * 12 + (4 + blk + 1))
                    ada_unit(n % RAW, a % 2, blk % 2)

                def s_wait(key):
                    k = S_AT[key]
                    dve.wait_ge(s_full, l * NSMALL + (PRE_SMALL + k + 1))
                    return small[k % 2], s_free[k % 2]

                def ada_out(blk):
                    bank, free = s_wait(("ada", blk, 0))
                    chunk, half = blk // 2, blk % 2
                    if chunk in GATE_CHUNKS:
                        if half == 0:
                            dve.wait_ge(g_in, l * 32 + (16 if chunk == GATE_CHUNKS[0] else 32))
                        g = g_row[:, 512 * half:512 * half + 512]
                        dve.tensor_tensor(g, bank[:, :], g, ALU.add).then_inc(free, 1)
                        return
                    if chunk < NEXT_CHUNKS:
                        dst_row = chunk
                        b0 = (DEPTH - 1) * 48 + 8 * chunk + 4 * half
                        bias = b_col[:, b0:b0 + 4]
                    else:
                        dst_row = chunk - 1
                        bias = b_col[:, bass.ds(l * 48 + (8 * chunk + 4 * half), 4)]
                    own.link(column(S_AT[("ada", blk, 0)], dst_row, half, bias))
                    dve.sem_inc(free, 1)
                    dve.sem_inc(mod_ready, 1)

                def h_lows():
                    def run(which):
                        for j in range(4):
                            dve.wait_ge(h_hi_ready, l * 8 + (4 * which + j + 1))
                            dve.tensor_tensor(h_lo[:, 2 * j:2 * j + 2, :], h_f32[:, 2 * j:2 * j + 2, :],
                                              h_hi[:, 2 * j:2 * j + 2, :].bitcast(F32), ALU.subtract)\
                                .then_inc(h_lo_ready, 1)
                    return run

                h_low = h_lows()

                def forget_logits():
                    dve.wait_ge(tr_full, l * NTR + 2)
                    dve.tensor_tensor(f_v[:, :, :], turn[:, 0:8].rearrange("p (r h) -> p r h", r=RB),
                                      fb_cur[:, :].unsqueeze(1).broadcast_to([P, RB, 4]), ALU.add).then_inc(f_ready, 1)
                    dve.wait_ge(f_ready, l + 1)
                    dve.sem_inc(tr_free, 1)

                def log_forget():
                    dve.wait_ge(log_ready, l * 5 + 1)
                    own.link(dve.scalar_tensor_tensor(out=f_lf[:, :, :], in0=f_v[:, :, :], scalar=0.0, in1=f_l[:, :, :],
                                                      op0=ALU.min, op1=ALU.subtract))
                    dve.tensor_copy(lf_b[:, :, :], f_lf[:, :, :].rearrange("p r h -> p (r h)").unsqueeze(2)
                                    .broadcast_to([P, 8, P])).then_inc(lf_ready, 1)

                def slot_wait(i, j):
                    if j == 0 and i >= 4:
                        dve.wait_ge(tr_full, l * NTR + (TR.index(("p", i - 4)) + 1))

                def head_first(i):
                    b, h = HEADS[i]
                    for j in range(2 if b == "A" else 1):
                        k = K_AT[(i, j)]
                        bank, free = s_wait(("s", i, j))
                        slot_wait(i, j)
                        pr = probs[:, prob_slot(i, j), :]
                        if b == "B":
                            own.link(dve.tensor_tensor(pr, bank[:, 0:384], tab[:, C_STRICT:C_STRICT + 384], ALU.add))
                            dve.sem_inc(z_ready, 1)
                            dve.sem_inc(free, 1)
                            continue
                        m0 = C_DIL if b == "C" else C_CAUSAL
                        scale = 32.0 ** -0.5 if b == "A" else 1.0
                        dve.sem_inc(seen_dve, 1)
                        own.mark(dve.tensor_tensor_reduce(
                            pr[:, 0:P], bank[:, 0:P], tab[:, m0:m0 + P], scale, -3e38, ALU.add, ALU.max,
                            tmax[:, k, 0:1]))
                        a2 = own.mark(dve.tensor_tensor_reduce(
                            pr[:, P:3 * P], bank[:, P:3 * P], tab[:, m0 + P:m0 + 3 * P], scale, -3e38, ALU.add,
                            ALU.max, tmax[:, k, 1:2]))
                        own.after(a2)
                        dve.sem_inc(free, 1)
                        dve.tensor_scalar(nmax[:, k, :], tmax[:, k, :], -1.0, None, ALU.mult).then_inc(sm_ready, 1)

                def exp_count(i):
                    return sum({"B": 1, "D": 2, "A": 4, "C": 2}[HEADS[n][0]] for n in range(i + 1))

                def head_second(i):
                    b, h = HEADS[i]
                    if b == "B":
                        k = K_AT[(i, 0)]
                        pr, sp_ = probs[:, prob_slot(i, 0), :], soft[:, h % 2, :]
                        cs = sp_
                        dve.wait_ge(log_ready, l * 5 + (1 + h + 1))
                        own.link(dve.scalar_tensor_tensor(out=sp_, in0=pr, scalar=0.0, in1=sp_, op0=ALU.max, op1=ALU.add))
                        dve.tensor_tensor_scan(cs[:, 0:P][:, ::-1], ones[:, 0:P], sp_[:, 0:P][:, ::-1], 0.0,
                                               ALU.mult, ALU.add)
                        own.link(dve.tensor_tensor_scan(cs[:, P:3 * P][:, ::-1], ones[:, 0:2 * P],
                                                        sp_[:, P:3 * P][:, ::-1], 0.0, ALU.mult, ALU.add))
                        dve.tensor_tensor(pr, pr, cs, ALU.subtract).then_inc(la_ready, 1)
                        return
                    dve.wait_ge(exp_ready, l * 36 + exp_count(i))
                    if b != "A":
                        o = ORDER.index(b)
                        own.link(dve.reciprocal(rden[:, o, :, h], den[:, K_AT[(i, 0)], :]))
                        return
                    k0, k1 = K_AT[(i, 0)], K_AT[(i, 1)]
                    p0, p1 = probs[:, prob_slot(i, 0), :], probs[:, prob_slot(i, 1), :]
                    dve.reciprocal(rsub[:, h, 0, :], den[:, k0, :])
                    own.link(dve.reciprocal(rsub[:, h, 1, :], den[:, k1, :]))
                    own.link(dve.tensor_scalar(rsub[:, h, 1, :], rsub[:, h, 1, :], lam_cur[:, 0:1], None, ALU.mult))
                    dve.tensor_scalar(p1[:, 0:P], p1[:, 0:P], rsub[:, h, 1, 0:1], None, ALU.mult)
                    own.link(dve.tensor_scalar(p1[:, P:3 * P], p1[:, P:3 * P], rsub[:, h, 1, 1:2], None, ALU.mult))
                    dve.scalar_tensor_tensor(out=p0[:, 0:P], in0=p0[:, 0:P], scalar=rsub[:, h, 0, 0:1], in1=p1[:, 0:P],
                                             op0=ALU.mult, op1=ALU.add)
                    dve.scalar_tensor_tensor(out=p0[:, P:3 * P], in0=p0[:, P:3 * P], scalar=rsub[:, h, 0, 1:2],
                                             in1=p1[:, P:3 * P], op0=ALU.mult, op1=ALU.add).then_inc(mix_ready, 1)

                def rope(b):
                    n, r0, half = (16, 0, CA) if b == "A" else (8, CA, CC)
                    dve.wait_ge(mm_free[0 if b == "A" else 1], l * (NMM // 2) + (1 + 3))
                    v = qk_rows[:, :, :, :].rearrange("p r c (h d) -> p r (c h) d", d=BW * 2 // n)
                    x1, x2 = v[:, :, :, 0:half], v[:, :, :, half:2 * half]
                    cos = cos_t[:, :, r0:r0 + half].unsqueeze(2).broadcast_to([P, RB, n, half])
                    sin = sin_t[:, :, r0:r0 + half].unsqueeze(2).broadcast_to([P, RB, n, half])
                    t = [rot[:, i, :].rearrange("p (r h d) -> p r h d", r=RB, h=n) for i in range(4)]
                    dve.tensor_tensor(t[0], x1, cos, ALU.mult)
                    dve.tensor_tensor(t[1], x2, sin, ALU.mult)
                    dve.tensor_tensor(t[2], x2, cos, ALU.mult)
                    own.link(dve.tensor_tensor(t[3], x1, sin, ALU.mult))
                    dve.tensor_tensor(x1, t[0], t[1], ALU.subtract)
                    dve.tensor_tensor(x2, t[2], t[3], ALU.add).then_inc(rope_ready, 1)

                def branch_rows(o):
                    b = ORDER[o]
                    dve.wait_ge(ov_full, l * 4 + (o + 1))
                    if o >= 1:
                        dve.wait_ge(s_full, l * NSMALL + (PRE_SMALL + S_AT[("o", o - 1, 0)] + 1))
                    src = ov[:, :].rearrange("p (r h d) -> p r h d", r=RB, h=4)
                    if b in "CD":
                        ins = dve.tensor_tensor(o_rows[:, :, :, :], src,
                                                rden[:, o, :, :].unsqueeze(3).broadcast_to([P, RB, 4, HD]), ALU.mult)
                    else:
                        ins = dve.tensor_copy(o_rows[:, :, :, :], src)
                    own.link(ins)
                    dve.sem_inc(ov_free, 1)
                    if b == "A":
                        own.link(dve.tensor_tensor(o_sq[:, :, :, :], o_rows[:, :, :, :], o_rows[:, :, :, :], ALU.mult))
                        own.link(dve.tensor_reduce(ve[:, 0:8].rearrange("p (r h) -> p r h", r=RB), o_sq[:, :, :, :],
                                                   AX_X, ALU.add))
                        own.link(dve.tensor_scalar(ve[:, 0:8], ve[:, 0:8], 1.0 / HD, EPS, ALU.mult, ALU.add))
                        dve.sem_inc(var_ready, 1)
                        dve.wait_ge(rstd_ready, l * 3 + 1)
                        own.link(dve.tensor_tensor(
                            o_rows[:, :, :, :], o_rows[:, :, :, :],
                            rstd[:, 0:8].rearrange("p (r h) -> p r h", r=RB).unsqueeze(3).broadcast_to([P, RB, 4, HD]),
                            ALU.mult))
                        own.link(dve.tensor_tensor(
                            o_rows[:, :, :, :].rearrange("p r h d -> p (r h) d"),
                            o_rows[:, :, :, :].rearrange("p r h d -> p (r h) d"),
                            sub_cur[:, :].unsqueeze(1).broadcast_to([P, 8, HD]), ALU.mult))
                    dve.sem_inc(o_ready, 1)

                def branch_lo(o):
                    bank, free = s_wait(("o", o, 0))
                    n = "ABCD".index(ORDER[o])
                    dve.wait_ge(br_hi_ready, l * 4 + (o + 1))
                    dve.tensor_tensor(br_lo[:, 2 * n:2 * n + 2, :], bank[:, :].rearrange("p (t q) -> p t q", t=2),
                                      br_hi[:, 2 * n:2 * n + 2, :].bitcast(F32), ALU.subtract).then_inc(br_lo_ready, 1)
                    dve.wait_ge(br_lo_ready, l * 4 + (o + 1))
                    dve.sem_inc(free, 1)

                def merge(dt):
                    n = MM_AT[(U_BR + dt // 2, dt % 2)]
                    dve.wait_ge(mm_full, l * NMM + (ONE + n + 1))
                    g = gated[:, dt % 2, :, :]
                    if dt >= 2:
                        dve.wait_ge(m_lo_ready, l * KT + (dt - 1))
                    own.link(dve.scalar_tensor_tensor(out=g, in0=gates[:, :, dt, :], scalar=1.0, in1=mm[n % 2][:, :, :],
                                                      op0=ALU.add, op1=ALU.mult))
                    dve.sem_inc(mm_free[n % 2], 1)
                    own.link(dve.tensor_tensor(g[:, 0:2, :], g[:, 0:2, :], g[:, 2:4, :], ALU.add))
                    dve.tensor_tensor(g[:, 0, :], g[:, 0, :], g[:, 1, :], ALU.add).then_inc(merged_ready, 1)

                def merged_lo(dt):
                    dve.wait_ge(m_hi_ready, l * KT + (dt + 1))
                    dve.scalar_tensor_tensor(out=h_lo[:, dt, :], in0=gated[:, dt % 2, 0, :], scalar=0.5,
                                             in1=h_hi[:, dt, :].bitcast(F32), op0=ALU.mult, op1=ALU.subtract)\
                        .then_inc(m_lo_ready, 1)

                def residual(u, ob):
                    n = MM_AT[(u, 0)]
                    dve.wait_ge(mm_full, l * NMM + (ONE + n + 1))
                    bank = mm[n % 2][:, :, :].rearrange("p (r a) q -> p r (a q)", r=RB)
                    t = gated[:, 0, :, :].rearrange("p (r a) q -> p r (a q)", r=RB)
                    xs = xr[:, :, 512 * ob:512 * ob + 512]
                    dve.wait_ge(m_lo_ready, l * KT + KT)
                    own.link(dve.tensor_tensor(t, bank, g_row[:, 512 * ob:512 * ob + 512].unsqueeze(1)
                                               .broadcast_to([P, RB, 512]), ALU.mult))
                    dve.sem_inc(mm_free[n % 2], 1)
                    own.link(dve.scalar_tensor_tensor(out=xs, in0=xs, scalar=ALPHA, in1=t, op0=ALU.mult, op1=ALU.add))
                    for r in range(RB):
                        ins = dve.bn_stats(stats[:, r, ob, :], xs[:, r, :])
                    own.link(ins)

                def layer_norm(which):
                    dve.sem_inc(seen_dve, 1)
                    for r in range(RB):
                        ins = dve.bn_aggr(mv[:, r, :], stats[:, r, :, :].rearrange("p a b -> p (a b)"))
                    own.link(ins)
                    dve.tensor_scalar(ve[:, 0:2], mv[:, :, 1], EPS, None, ALU.add).then_inc(var_ready, 1)
                    dve.wait_ge(rstd_ready, l * 3 + (which + 2))
                    dve.wait_ge(ln_in, l * 64 + 32 * (which + 1))
                    for r in range(RB):
                        own.link(dve.tensor_scalar(xr[:, r, :], xr[:, r, :], mv[:, r, 0:1], rstd[:, r:r + 1],
                                                   ALU.subtract, ALU.mult))
                    for t, op in ((ln_g, ALU.mult), (ln_b, ALU.add)):
                        own.link(dve.tensor_tensor(xr[:, :, :], xr[:, :, :],
                                                   t[:, :].unsqueeze(1).broadcast_to([P, RB, D]), op))
                    dve.sem_inc(x_done, 1)

                def conv_taps(m):
                    n = MM_AT[(U_UP + 2 * m + 1, 0)]
                    bank, y = mm[n % 2], (y_a, y_g)[m % 2]
                    dve.wait_ge(base_ready, l * 32 + 4 * (m + 1))
                    for tap in (1, 0):
                        shift = 2 - tap
                        for t in range(4):
                            f = 16 * (m % 2) + 4 * (m // 2) + t
                            ins = dve.scalar_tensor_tensor(
                                out=y[:, t, shift:SEQ], in0=bank[:, t, 0:SEQ - shift],
                                scalar=cv[:, 32 * tap + f:32 * tap + f + 1], in1=y[:, t, shift:SEQ],
                                op0=ALU.mult, op1=ALU.add)
                        own.link(ins)
                    dve.sem_inc(mm_free[n % 2], 1)

                def ffn_a(j):
                    dve.wait_ge(tanh_ready, l * 4 + (j + 1))
                    own.link(dve.scalar_tensor_tensor(out=y_a[:, :, :], in0=th[:, :, :], scalar=1.0, in1=y_a[:, :, :],
                                                      op0=ALU.add, op1=ALU.mult))

                def ffn_product():
                    dve.scalar_tensor_tensor(out=y_g[:, :, :], in0=y_a[:, :, :], scalar=0.5, in1=y_g[:, :, :],
                                             op0=ALU.mult, op1=ALU.mult).then_inc(prod_ready, 1)

                def ffn_lo(j):
                    dve.wait_ge(act_hi_ready, l * 4 + (j + 1))
                    dve.tensor_tensor(act_lo[:, 4 * j:4 * j + 4, :], y_g[:, :, :],
                                      act_hi[:, 4 * j:4 * j + 4, :].bitcast(F32), ALU.subtract)\
                        .then_inc(act_lo_ready, 1)

                lo(0)
                lo(1)
                own.link(dve.tensor_copy(wf_hi[:, :, :], wf[:, bass.ds(l * KT, KT), :]))
                dve.tensor_tensor(wf_lo[:, :, :], wf[:, bass.ds(l * KT, KT), :], wf_hi[:, :, :].bitcast(F32),
                                  ALU.subtract).then_inc(wf_ready, 1)
                dve.tensor_copy(lam_cur[:, :], lam_n[:, bass.ds(l, 1)])
                dve.tensor_copy(sub_cur[:, :].unsqueeze(1), sub_g[:, bass.ds(l, 1), :])
                own.link(dve.tensor_copy(fb_cur[:, :].unsqueeze(1), f_b[:, bass.ds(l, 1), :]))
                h_low(0)
                lo(2)

                for s in range(2, UNITS + 1):
                    if s + 1 < UNITS:
                        lo(s + 1)
                    if U_UP + 3 <= s <= U_DOWN + 1 and s % 2:
                        m = (s - U_UP - 3) // 2
                        (ffn_lo if m % 2 else ffn_a)(m // 2)
                    if s in ADA_STEPS:
                        ada(ADA_STEPS.index(s))
                    if s == 2:
                        forget_logits()
                    if s == 3:
                        log_forget()
                    if s in (10, 14):
                        rope("A" if s == 10 else "C")
                    if 0 <= s - 7 < 16:
                        head_second(s - 7)
                    if 0 <= s - 6 < 16:
                        head_first(s - 6)
                    if s in (13, 17, 21, 25):
                        branch_rows((s - 13) // 4)
                    if s - 1 in OT_AFTER:
                        branch_lo(OT_AFTER[s - 1])
                    if s - 1 in ADA_AFTER:
                        ada_out(ADA_AFTER[s - 1])
                    if U_BR < s <= U_BR + 4:
                        dt = 2 * (s - U_BR - 1)
                        merge(dt)
                        merge(dt + 1)
                        merged_lo(dt)
                        merged_lo(dt + 1)
                    if s == U_O + 3:
                        residual(U_O + 2, 0)
                    if s == U_O + 4:
                        residual(U_O + 3, 1)
                        layer_norm(0)
                        h_low(1)
                    if U_UP + 2 <= s <= U_DOWN and s % 2 == 0:
                        m = (s - U_UP) // 2 - 1
                        conv_taps(m)
                        if m % 2:
                            ffn_product()
                        else:
                            dve.sem_inc(conv_ready, 1)
                    if s == U_DOWN + 7:
                        residual(U_DOWN + 6, 0)
                    if s == U_DOWN + 8:
                        residual(U_DOWN + 7, 1)
                        layer_norm(1)
                own.leave()

        @block.tensor
        def _(pe):
            for s in (*mm_free, *s_free, ov_free, mm_full, unit_done):
                pe.sem_inc(s, 1)
            pe.wait_ge(small_in, 48)
            pe.wait_ge(s_free[0], 1)
            pe.transpose(small[0][:, 0:8], c_rows[:, :], idn[0:8, 0:8]).then_inc(s_full, 1)
            pe.wait_ge(s_free[1], 1)
            pe.transpose(small[1][:, 0:96], b_rows[:, :], idn[0:96, 0:96]).then_inc(s_full, 1)

            def ada_columns(bank, buf):
                for t in range(4):
                    ins = pe.matmul(bank[:, t:t + 1], acc[:, buf, P * t:P * t + P], ones[:, 0:1], start=True, stop=True)
                ins.then_inc(s_full, 1)

            for k in range(4):
                pe.wait_ge(acc_ready, k + 1)
                pe.wait_ge(s_free[k % 2], k // 2 + 2)
                ada_columns(small[k % 2], k % 2)
            pe.wait_ge(x_in, 16 * 9)

            with pe.Fori(0, DEPTH) as l:
                def s_take(key):
                    k = S_AT[key]
                    pe.wait_ge(s_free[k % 2], l * (NSMALL // 2) + (PRE_SMALL // 2 + k // 2 + 1))
                    return small[k % 2]


                def turn_x(which):
                    pe.wait_ge(x_done, l * 2 + (ONE + which))
                    for j in range(4):
                        bank = s_take(("x", which, j))
                        for t in range(2):
                            for r in range(RB):
                                ft = 2 * j + t
                                ins = pe.transpose(bank[:, SEQ * t + P * r:SEQ * t + P * r + P],
                                                   xr[:, r, P * ft:P * ft + P], idn)
                        ins.then_inc(s_full, 1)

                def mm_take(n):
                    pe.wait_ge(mm_free[n % 2], l * (NMM // 2) + (n // 2 + 1))
                    return mm[n % 2]

                def passes(out, stat, mov, first, last):
                    pairs = ((stat[0], mov[0]), (stat[0], mov[1]), (stat[1], mov[0]))
                    for i, (a, b) in enumerate(pairs):
                        ins = pe.matmul(out, a, b, start=first and i == 0, stop=last and i == 2,
                                        skip_group_check=True)
                    return ins

                def take_unit(w):
                    pe.wait_ge(hi_ready, l * UNITS + (w + 1))
                    pe.wait_ge(lo_ready, l * UNITS + (ONE + w + 1))
                    return w % SPLIT

                def features_or_rows(w, group, form, src, kh):
                    s = take_unit(w)
                    bank = mm_take(group) if kh == 0 else mm[group % 2]
                    hi, lo = (t[:, s, :].rearrange("p (k n) -> p k n", k=4) for t in (w_hi, w_lo))
                    for half in range(2):
                        for t in range(2):
                            for kk in range(4):
                                k = 4 * kh + kk
                                c0 = 256 * half
                                if form[half] == "T":
                                    sl = slice(c0 + P * t, c0 + P * t + P)
                                    st = (hi[:, kk, sl], lo[:, kk, sl])
                                    mv_ = (src[0][:, k, :], src[1][:, k, :])
                                else:
                                    st = tuple(a[:, k, P * t:P * t + P] for a in src)
                                    mv_ = (hi[:, kk, c0:c0 + 256], lo[:, kk, c0:c0 + 256])
                                ins = passes(bank[:, 2 * half + t, :], st, mv_, first=(k == 0 and t == 0), last=(k == 7))
                    ins.then_inc(mm_full if kh == 1 else unit_done, 1)

                def rows(w, group, src, k0, first, last):
                    s = take_unit(w)
                    bank = mm_take(group) if first else mm[group % 2]
                    out = bank[:, :, :].rearrange("p (r a) q -> p r (a q)", r=RB)
                    hi, lo = (t[:, s, :].rearrange("p (k n) -> p k n", k=4) for t in (w_hi, w_lo))
                    for r in range(RB):
                        for kk in range(4):
                            k = k0 + kk
                            ins = passes(out[:, r, :], tuple(a[:, k, P * r:P * r + P] for a in src),
                                         (hi[:, kk, :], lo[:, kk, :]), first=first and kk == 0, last=last and kk == 3)
                    ins.then_inc(mm_full if last else unit_done, 1)

                def branches(w):
                    s = take_unit(w)
                    hi, lo = (t[:, s, :].rearrange("p (k n) -> p k n", k=8) for t in (w_hi, w_lo))
                    for t in range(2):
                        n = MM_AT[(w, t)]
                        bank = mm_take(n)
                        for br in range(NBR):
                            for c2 in range(2):
                                k = 2 * br + c2
                                sl = slice(P * t, P * t + P)
                                ins = passes(bank[:, br, :], (hi[:, k, sl], lo[:, k, sl]),
                                             (br_hi[:, k, :], br_lo[:, k, :]), first=(c2 == 0), last=(c2 == 1))
                        ins.then_inc(mm_full, 1)

                def forget(src):
                    pe.wait_ge(wf_ready, l + 1)
                    pe.wait_ge(tr_free, l * 2 + 1)
                    for r in range(RB):
                        for k in range(KT):
                            ins = passes(turn[:, 4 * r:4 * r + 4], tuple(a[:, k, P * r:P * r + P] for a in src),
                                         (wf_hi[:, k, :], wf_lo[:, k, :]), first=(k == 0), last=(k == KT - 1))
                    ins.then_inc(tr_full, 1)

                def scores(i):
                    b, h = HEADS[i]
                    st = {"B": 0, "D": 1, "A": 0, "C": 1}[b]
                    if b == "D" and h == 0:
                        pe.wait_ge(lf_ready, l + 1)
                    if b in "AC" and h == 0:
                        for j in range(2):
                            k = S_AT[("qk", b, j)]
                            pe.wait_ge(s_free[k % 2], l * (NSMALL // 2) + (PRE_SMALL // 2 + k // 2 + 2))
                    if h == 0 and b in "BD":
                        pe.wait_ge(mm_free[1], l * (NMM // 2) + (1 + (1 if b == "B" else 2)))
                    for j in range(2 if b == "A" else 1):
                        bank = s_take(("s", i, j))
                        dd = 32 if b == "A" else 64
                        hh = 2 * h + j if b == "A" else h
                        per = P // dd
                        p0, ft = dd * (hh % per), hh // per
                        q, k = q_T[st][p0:p0 + dd, ft, :], k_T[st][p0:p0 + dd, ft, :]
                        for blk in range(RB):
                            out = bank[:, P * blk:P * blk + P * (blk + 1)]
                            ins = pe.matmul(out, q[:, P * blk:P * blk + P], k[:, 0:P * (blk + 1)], start=True,
                                            stop=(b != "D"))
                            if b == "D":
                                for jt in range(blk + 1):
                                    ins = pe.matmul(out, lf_b[:, 4 * jt + h, :],
                                                    tab[:, C_NU + SEQ * jt:C_NU + SEQ * jt + P * (blk + 1)],
                                                    start=False, stop=(jt == blk))
                        ins.then_inc(s_full, 1)

                def turn_probs(i):
                    b, h = HEADS[i]
                    if b == "A":
                        pe.wait_ge(mix_ready, l * 4 + (h + 1))
                    else:
                        count = sum({"B": 1, "D": 2, "A": 4, "C": 2}[HEADS[n][0]] for n in range(i + 1))
                        pe.wait_ge(exp_ready, l * 36 + count)
                    if i == 0:
                        pe.wait_ge(tr_free, l * 2 + 2)
                    else:
                        pe.wait_ge(pt_ready, l * 16 + (ONE + i))
                    pr = probs[:, prob_slot(i, 0), :]
                    for t in range(3):
                        ins = pe.transpose(turn[:, P * t:P * t + P], pr[:, P * t:P * t + P], idn)
                    ins.then_inc(tr_full, 1)

                def weigh(i):
                    b, h = HEADS[i]
                    o = i // 4
                    pe.wait_ge(pt_ready, l * 16 + (ONE + i + 1))
                    if h == 0:
                        pe.wait_ge(ov_free, l * 4 + (o + 1))
                    pt, v = p_T[:, i % 2, :], v_of[b]
                    cols = slice(HD * h, HD * h + HD)
                    out0, out1 = ov[:, HD * h:HD * h + HD], ov[:, BW + HD * h:BW + HD * h + HD]
                    pe.matmul(out0, pt[:, 0:P], v[:, 0, cols], start=True, stop=True)
                    pe.matmul(out1, pt[:, P:2 * P], v[:, 0, cols], start=True, stop=False)
                    pe.matmul(out1, pt[:, 2 * P:3 * P], v[:, 1, cols], start=False, stop=True).then_inc(pv_done, 1)
                    if h == 3:
                        pe.wait_ge(pv_done, l * 16 + (i + 1))
                        pe.sem_inc(ov_full, 1)

                def turn_qk(b):
                    pe.wait_ge(rope_ready, l * 2 + (1 if b == "A" else 2))
                    for j in range(2):
                        bank = s_take(("qk", b, j))
                        for ft in range(2):
                            for r in range(RB):
                                ins = pe.transpose(bank[:, SEQ * ft + P * r:SEQ * ft + P * r + P],
                                                   qk_rows[:, r, j, P * ft:P * ft + P], idn)
                        ins.then_inc(s_full, 1)

                def turn_o(o):
                    pe.wait_ge(o_ready, l * 4 + (o + 1))
                    bank = s_take(("o", o, 0))
                    flat = o_rows[:, :, :, :].rearrange("p r h d -> p r (h d)")
                    for c2 in range(2):
                        for r in range(RB):
                            ins = pe.transpose(bank[:, SEQ * c2 + P * r:SEQ * c2 + P * r + P],
                                               flat[:, r, P * c2:P * c2 + P], idn)
                    ins.then_inc(s_full, 1)

                def ada_sum(blk):
                    pe.wait_ge(acc_ready, l * 12 + (4 + blk + 1))
                    bank = s_take(("ada", blk, 0))
                    if blk // 2 in GATE_CHUNKS:
                        pe.matmul(bank[:, :], ones[:, 0:P], acc[:, blk % 2, :], start=True, stop=True)\
                            .then_inc(s_full, 1)
                    else:
                        ada_columns(bank, blk % 2)

                h = (h_hi, h_lo)
                turn_x(0)
                pe.wait_ge(cv_in, l * 32 + 32)
                pe.wait_ge(pt_ready, l * 16 + ONE)
                pe.transpose(turn[:, 0:P], cv_rows[:, :], idn).then_inc(tr_full, 1)

                for u in range(UNITS):
                    if u < U_BR:
                        form = IN_BLOCKS[u // 2][1] if u < U_GATE else "TT"
                        if u < 2:
                            pe.wait_ge(h_hi_ready, l * 8 + 2 * (u + 1))
                            pe.wait_ge(h_lo_ready, l * 8 + 2 * (u + 1))
                        features_or_rows(u, MM_AT[(u | 1, 0)], form, h, u % 2)
                    elif u < U_O:
                        if u == U_BR:
                            pe.wait_ge(br_hi_ready, l * 4 + 4)
                            pe.wait_ge(br_lo_ready, l * 4 + 4)
                        branches(u)
                    elif u < U_UP:
                        ob, kb = O_ORDER[u - U_O]
                        if ob == 0:
                            pe.wait_ge(m_hi_ready, l * KT + 4 * (kb + 1))
                            pe.wait_ge(m_lo_ready, l * KT + 4 * (kb + 1))
                        rows(u, MM_AT[(U_O + 2 + ob, 0)], h, 4 * kb, kb == 0, kb == 1)
                    elif u < U_DOWN:
                        if u == U_UP:
                            turn_x(1)
                        if u < U_UP + 2:
                            pe.wait_ge(h_hi_ready, l * 8 + 4 + 2 * (u - U_UP + 1))
                            pe.wait_ge(h_lo_ready, l * 8 + 4 + 2 * (u - U_UP + 1))
                        features_or_rows(u, MM_AT[(u | 1, 0)], "TT", h, u % 2)
                    else:
                        ob, kb = DOWN_ORDER[u - U_DOWN]
                        if ob == 0:
                            pe.wait_ge(act_hi_ready, l * 4 + (kb + 1))
                            pe.wait_ge(act_lo_ready, l * 4 + (kb + 1))
                        rows(u, MM_AT[(U_DOWN + 6 + ob, 0)], (act_hi, act_lo), 4 * kb, kb == 0, kb == 3)
                    if u == 1:
                        forget(h)
                    if score_head(u) is not None:
                        scores(score_head(u))
                    if 0 <= u - 8 < 16:
                        turn_probs(u - 8)
                    if 0 <= u - 9 < 16:
                        weigh(u - 9)
                    if u in QK_AFTER:
                        turn_qk(QK_AFTER[u])
                    if u in OT_AFTER:
                        turn_o(OT_AFTER[u])
                    if u in ADA_AFTER:
                        ada_sum(ADA_AFTER[u])


_INS = ["x", "c", "positions", "w_ada", "b_ada", "w_in", "lam_q1", "lam_k1", "lam_q2", "lam_k2", "subln_g", "forget_b",
        "w_branch", "w_o", "ln1_g", "ln1_b", "w_up", "conv_w", "conv_b", "w_down", "ln2_g", "ln2_b"]


def kernel(**inputs):
    import numpy as _np
    import concourse.bacc as _bacc
    from concourse import mybir as _mybir
    from concourse.bass_utils import run_bass_kernel_spmd as _run

    nc = _bacc.Bacc("TRN2", target_bir_lowering=False, num_devices=1)
    arrays, args = {}, []
    for name in _INS:
        a = _np.ascontiguousarray(inputs[name])
        arrays[f"in_{name}_dram"] = a
        args.append(nc.dram_tensor(f"in_{name}_dram", a.shape, _mybir.dt.from_np(a.dtype), kind="ExternalInput").ap())
    t = constants()
    arrays["table_dram"] = t
    args.append(nc.dram_tensor("table_dram", t.shape, _mybir.dt.float32, kind="ExternalInput").ap())
    o = nc.dram_tensor("out_0_dram", (1, SEQ, D), _mybir.dt.float32, kind="ExternalOutput").ap()
    build(nc, *args, o)
    return _run(nc, [arrays], core_ids=[0]).results[0]["out_0_dram"]
```

```python
import math
from contextlib import ExitStack

import numpy as np

import concourse.bass as bass
from concourse import mybir

ALU = mybir.AluOpType
ACT = mybir.ActivationFunctionType
AX_X = mybir.AxisListType.X
F32 = mybir.dt.float32
F32R = mybir.dt.float32r
I32 = mybir.dt.int32

P = 128
D = 1024
SEQ = 256
DEPTH = 2
RB = SEQ // P
KT = D // P
DFF = 2048
FT = 2 * DFF // P
HD = 64
BW = 4 * HD
NBR = 4
EPS = 1e-5
ALPHA = (2.0 * DEPTH) ** 0.25
NEG = -1e30
GATE0 = 12 * BW + 4
CA, CC = 4, 8
THETA = 500000.0

RAW = 4
SPLIT = 3
UNITS = 60
U_IN, U_GATE, U_BR, U_O, U_UP, U_DOWN = 0, 12, 28, 32, 36, 52
IN_BLOCKS = [(2 * BW, "RT"), (4 * BW, "TR"), (8 * BW, "RT"), (10 * BW, "TR"), (0, "RR"), (6 * BW, "RR")]
O_ORDER = [(0, 0), (1, 0), (0, 1), (1, 1)]
DOWN_ORDER = [(0, 0), (0, 1), (0, 2), (1, 0), (1, 1), (1, 2), (0, 3), (1, 3)]
ORDER = "BDAC"
HEADS = [(b, h) for b in ORDER for h in range(4)]
ADA_STEPS = [2, 3, 4, 5, 6, 8, 10, 11, 12, 14, 16, 17, 18, 20, 21, 22, 23, 24, 25, 27, 39, 43, 47, 51]
NEXT_CHUNKS = 2
GATE_CHUNKS = (2, 5)
STREAM = []
for _w in range(UNITS):
    STREAM.append(("w", _w))
    if _w - 2 in ADA_STEPS:
        STREAM.append(("ada", ADA_STEPS.index(_w - 2)))
NSTREAM = len(STREAM)
AT = {u: n for n, u in enumerate(STREAM)}
PRE_ADA = 8
assert NSTREAM % RAW == 0 and PRE_ADA % RAW == 0 and UNITS % SPLIT == 0

MM_GROUPS = [(u, 0) for u in range(1, 28, 2)] + [(28 + q, t) for q in range(4) for t in range(2)] \
    + [(34, 0), (35, 0)] + [(u, 0) for u in range(37, 52, 2)] + [(58, 0), (59, 0)]
NMM = len(MM_GROUPS)
MM_AT = {g: n for n, g in enumerate(MM_GROUPS)}
assert NMM % 2 == 0

QK_AFTER = {11: ("A", 0), 12: ("A", 1), 15: ("C", 0), 16: ("C", 1)}
OT_AFTER = {14: 0, 18: 1, 22: 2, 25: 3}
ADA_AFTER = {ADA_STEPS[2 * i + 1] + 1: i for i in range(12)}


def score_head(u):
    return u - 5 if 5 <= u < 21 else None


def small_bank_uses():
    uses = [("x", 0, j) for j in range(4)]
    for u in range(UNITS):
        i = score_head(u)
        if i is not None:
            uses += [("s", i, j) for j in range(2 if HEADS[i][0] == "A" else 1)]
        if u in QK_AFTER:
            uses += [("qk", *QK_AFTER[u])]
        if u in OT_AFTER:
            uses += [("o", OT_AFTER[u], 0)]
        if u in ADA_AFTER:
            uses += [("ada", ADA_AFTER[u], 0)]
        if u == U_UP - 1:
            uses += [("x", 1, j) for j in range(4)]
    return uses


SMALL = small_bank_uses()
NSMALL = len(SMALL)
S_AT = {k: n for n, k in enumerate(SMALL)}
PRE_BLOCKS = 3
PRE_SMALL = 6
assert NSMALL % 2 == 0
SCORES = [k for k in SMALL if k[0] == "s"]
K_AT = {k[1:]: n for n, k in enumerate(SCORES)}
NSC = len(SCORES)
PROBS = 5


def prob_slot(i, j):
    return i % 4 if j == 0 else 4


TR = [("cv", 0), ("f", 0)] + [("p", i) for i in range(16)]
NTR = len(TR)

LN_COL = 6 * DEPTH * KT

C_IDN = 0
C_FREQ = C_IDN + P
C_LI = C_FREQ + CA + CC
C_STRICT = C_LI + 2 * DEPTH
C_CAUSAL = C_STRICT + 3 * P
C_DIL = C_CAUSAL + 3 * P
C_NU = C_DIL + 3 * P
NCONST = C_NU + 2 * SEQ


def constants():
    t = np.zeros((P, NCONST), np.float32)
    t[:, C_IDN:C_IDN + P] = np.eye(P)
    q = np.arange(P)[:, None]
    for blk, base in ((0, 0), (1, P)):
        k = np.arange(P * (blk + 1))[None, :]
        dist = q + P * blk - k
        put = slice(base, base + P * (blk + 1))
        t[:, C_STRICT:C_STRICT + 3 * P][:, put] = np.where(dist > 0, 0.0, NEG)
        t[:, C_CAUSAL:C_CAUSAL + 3 * P][:, put] = np.where(dist >= 0, 0.0, NEG)
        count = sum(((dist >= 0) & (dist % dil == 0) & (dist <= window)).astype(int)
                    for window, dil in ((128, 1), (512, 4), (2048, 16)))
        t[:, C_DIL:C_DIL + 3 * P][:, put] = np.where(count > 0, np.log(np.maximum(count, 1)), NEG)
    for jt in range(RB):
        j = np.arange(P)[:, None] + P * jt
        t[:, C_NU + SEQ * jt:C_NU + SEQ * (jt + 1)] = np.where(j <= np.arange(SEQ)[None, :], -1.0, 0.0)
    t[:, C_FREQ:C_FREQ + CA] = np.float32(THETA) ** (-2.0 * np.arange(CA, dtype=np.float32) / (2 * CA))
    t[:, C_FREQ + CA:C_FREQ + CA + CC] = np.float32(THETA) ** (-2.0 * np.arange(CC, dtype=np.float32) / (2 * CC))
    for l in range(DEPTH):
        li = 0.8 - 0.6 * math.exp(-0.3 * l)
        t[:, C_LI + l] = li
        t[:, C_LI + DEPTH + l] = 1.0 - li
    return t


ENDS = {u: n for (u, t), n in MM_AT.items()}
PLAIN = [u for u in range(UNITS) if u not in ENDS]
NPLAIN = len(PLAIN)


def unit_end(u):
    if u < 0:
        return True, 0
    return (True, ENDS[u] + 1) if u in ENDS else (False, PLAIN.index(u) + 1)


ONE = 1


class Own:

    def __init__(self, eng, sem, per_layer):
        self.eng, self.sem, self.per_layer = eng, sem, per_layer
        self.before, self.n, self.layer = 0, 0, 0

    def mark(self, ins):
        ins.then_inc(self.sem, 1)
        self.n += 1
        return self.n

    def after(self, n):
        self.eng.wait_ge(self.sem, self.layer * self.per_layer + (self.before + n))

    def link(self, ins):
        self.after(self.mark(ins))

    def enter(self, layer):
        self.before, self.n, self.layer = self.n, 0, layer

    def leave(self):
        assert self.n == self.per_layer, (self.sem, self.n)


ACT_OWN, DVE_OWN = 24, 238


def build(nc, x, c, positions, w_ada, b_ada, w_in, lam_q1, lam_k1, lam_q2, lam_k2, subln_g, forget_b, w_branch, w_o,
          ln1_g, ln1_b, w_up, conv_w, conv_b, w_down, ln2_g, ln2_b, table, out):
    with ExitStack() as ctx:
        def sb(name, shape, dt=F32):
            return ctx.enter_context(nc.sbuf_tensor(name, shape, dt))

        def sem(name):
            return ctx.enter_context(nc.semaphore(name))

        raw = sb("raw", [P, RAW, 2048])
        w_hi = sb("w_hi", [P, SPLIT, 2048], F32R)
        w_lo = sb("w_lo", [P, SPLIT, 2048], F32R)
        xr = sb("xr", [P, RB, D])
        h_hi = sb("h_hi", [P, KT, SEQ], F32R)
        h_lo = sb("h_lo", [P, KT, SEQ], F32R)
        br_hi = sb("br_hi", [P, KT, SEQ], F32R)
        br_lo = sb("br_lo", [P, KT, SEQ], F32R)
        with ExitStack() as phase:
            gates = phase.enter_context(nc.sbuf_tensor("gates", [P, 4, 8, SEQ], F32))
        with ExitStack() as phase:
            def early(name, shape):
                return phase.enter_context(nc.sbuf_tensor(name, shape, F32))
            early("gates_first_half", [P, 4096])
            q_T = [early(f"q_T{i}", [P, 2, SEQ]) for i in range(2)]
            k_T = [early(f"k_T{i}", [P, 2, SEQ]) for i in range(2)]
            qk_rows = early("qk_rows", [P, RB, 2, BW])
            v_b = early("v_b", [P, RB, BW])
            v_d = early("v_d", [P, RB, BW])
        act_hi = sb("act_hi", [P, 16, SEQ], F32R)
        act_lo = sb("act_lo", [P, 16, SEQ], F32R)
        v_a = sb("v_a", [P, RB, BW])
        v_c = sb("v_c", [P, RB, BW])
        v_of = {"A": v_a, "B": v_b, "C": v_c, "D": v_d}
        with ExitStack() as phase:
            h_f32 = phase.enter_context(nc.sbuf_tensor("h_f32", [P, KT, SEQ], F32))
        with ExitStack() as phase:
            c_rows = phase.enter_context(nc.sbuf_tensor("c_rows", [8, P], F32))
            b_rows = phase.enter_context(nc.sbuf_tensor("b_rows", [96, P], F32))
            ln_rows = phase.enter_context(nc.sbuf_tensor("ln_rows", [4 * DEPTH * KT, P], F32))
            lam_in = phase.enter_context(nc.sbuf_tensor("lam_in", [P, 4, DEPTH, 32], F32))
            ang_k = phase.enter_context(nc.sbuf_tensor("ang_k", [P, RB, CA + CC], F32))
        with ExitStack() as phase:
            y_a = phase.enter_context(nc.sbuf_tensor("y_a", [P, 4, SEQ], F32))
            y_g = phase.enter_context(nc.sbuf_tensor("y_g", [P, 4, SEQ], F32))
            th = phase.enter_context(nc.sbuf_tensor("th", [P, 4, SEQ], F32))
        with ExitStack() as phase:
            gated = phase.enter_context(nc.sbuf_tensor("gated", [P, 2, 4, SEQ], F32))
        probs = sb("probs", [P, PROBS, 384])
        with ExitStack() as phase:
            o_sq = phase.enter_context(nc.sbuf_tensor("o_sq", [P, RB, 4, HD], F32))
        soft = sb("soft", [P, 2, 384])
        p_T = sb("p_T", [P, 2, 384])
        o_rows = sb("o_rows", [P, RB, 4, HD])
        lf_b = sb("lf_b", [P, 8, P])
        acc = sb("acc", [P, 2, 512])
        g_row = sb("g_row", [P, D])
        ln_g = sb("ln_g", [P, D])
        ln_b = sb("ln_b", [P, D])
        tab = sb("tab", [P, NCONST])
        ones = sb("ones", [P, SEQ])
        sc_col = sb("sc_col", [P, KT])
        sc_tmp = sb("sc_tmp", [P, 2, KT])
        b_col = sb("b_col", [P, LN_COL + 4 * DEPTH * KT])
        mod = sb("mod", [P, 4, KT])
        mod_t = sb("mod_t", [P, 4])
        cv_rows = sb("cv_rows", [P, P])
        cv = sb("cv", [P, P])
        wf = sb("wf", [P, DEPTH * KT, 4])
        wf_hi = sb("wf_hi", [P, KT, 4], F32R)
        wf_lo = sb("wf_lo", [P, KT, 4], F32R)
        f_b = sb("f_b", [P, DEPTH, 4])
        f_v = sb("f_v", [P, RB, 4])
        f_l = sb("f_l", [P, RB, 4])
        f_lf = sb("f_lf", [P, RB, 4])
        pos_i = sb("pos_i", [P, RB], I32)
        pos_f = sb("pos_f", [P, RB])
        ang = sb("ang", [P, RB, CA + CC])
        ang_c = sb("ang_c", [P, RB, CA + CC])
        sin_t = sb("sin_t", [P, RB, CA + CC])
        cos_t = sb("cos_t", [P, RB, CA + CC])
        rot = sb("rot", [P, 4, 128])
        lam_s = sb("lam_s", [P, 2, DEPTH])
        lam_n = sb("lam_n", [P, DEPTH])
        sub_g = sb("sub_g", [P, DEPTH, HD])
        lam_cur = sb("lam_cur", [P, 1])
        sub_cur = sb("sub_cur", [P, HD])
        fb_cur = sb("fb_cur", [P, 4])
        nmax = sb("nmax", [P, NSC, 2])
        tmax = sb("tmax", [P, NSC, 2])
        den = sb("den", [P, NSC, 2])
        rden = sb("rden", [P, 4, RB, 4])
        rsub = sb("rsub", [P, 4, 2, 2])
        stats = sb("stats", [P, RB, 2, 6])
        mv = sb("mv", [P, RB, 2])
        ve = sb("ve", [P, 8])
        rstd = sb("rstd", [P, 8])
        nhalf = sb("nhalf", [P, 8])

        def psum(name):
            return ctx.enter_context(nc.psum_tensor(name, [P, 512], F32))

        mm = [ctx.enter_context(nc.psum_tensor(f"mm{i}", [P, 4, SEQ], F32)) for i in range(2)]
        small = [psum("small0"), psum("small1")]
        turn = psum("turn")
        ov = psum("ov")
        idn = tab[:, C_IDN:C_IDN + P]

        raw_in = [sem(f"raw_in{i}") for i in range(RAW)]
        hi_ready, lo_ready = sem("hi_ready"), sem("lo_ready")
        unit_done = sem("unit_done")
        mm_full = sem("mm_full")
        mm_free = [sem("mm_free0"), sem("mm_free1")]
        s_full = sem("s_full")
        s_free = [sem("s_free0"), sem("s_free1")]
        tr_full, tr_free = sem("tr_full"), sem("tr_free")
        ov_full, ov_free = sem("ov_full"), sem("ov_free")
        c_in, small_in, x_in, masks_in = sem("c_in"), sem("small_in"), sem("x_in"), sem("masks_in")
        sc_ready = sem("sc_ready")
        cv_in, g_in, ln_in = sem("cv_in"), sem("g_in"), sem("ln_in")
        h_hi_ready, h_lo_ready = sem("h_hi_ready"), sem("h_lo_ready")
        rope_ready = sem("rope_ready")
        f_ready, lf_ready, wf_ready = sem("f_ready"), sem("lf_ready"), sem("wf_ready")
        z_ready, log_ready, la_ready = sem("z_ready"), sem("log_ready"), sem("la_ready")
        sm_ready, exp_ready = sem("sm_ready"), sem("exp_ready")
        mix_ready = sem("mix_ready")
        pt_ready, pv_done = sem("pt_ready"), sem("pv_done")
        o_ready = sem("o_ready")
        br_hi_ready, br_lo_ready = sem("br_hi_ready"), sem("br_lo_ready")
        gate_ready, merged_ready = sem("gate_ready"), sem("merged_ready")
        m_hi_ready, m_lo_ready = sem("m_hi_ready"), sem("m_lo_ready")
        half_ready, acc_ready, mod_ready = sem("half_ready"), sem("acc_ready"), sem("mod_ready")
        cv_ready, base_ready, conv_ready = sem("cv_ready"), sem("base_ready"), sem("conv_ready")
        tanh_ready, prod_ready = sem("tanh_ready"), sem("prod_ready")
        act_hi_ready, act_lo_ready = sem("act_hi_ready"), sem("act_lo_ready")
        var_ready, rstd_ready = sem("var_ready"), sem("rstd_ready")
        x_done = sem("x_done")
        row0_full = sem("row0_full")
        affine_done, out_ready = sem("affine_done"), sem("out_ready")
        last_done, plain_ln = sem("last_done"), sem("plain_ln")
        pre_act, pre_dve, pre_pe = sem("pre_act"), sem("pre_dve"), sem("pre_pe")
        act_own, dve_own = sem("act_own"), sem("dve_own")
        seen_sp, seen_dve, seen_pool = sem("seen_sp"), sem("seen_dve"), sem("seen_pool")
        nhalf_ready, out_done = sem("nhalf_ready"), sem("out_done")

        def ktiles(w):
            return w.rearrange("l (k p) n -> p (l k) n", p=P)
        ada_v, in_v, o_v, up_v, down_v = (ktiles(w) for w in (w_ada, w_in, w_o, w_up, w_down))
        br_v = w_branch.rearrange("l n (k p) d -> p (l n k) d", p=P)

        def wide(slot):
            return raw[:, slot, :].rearrange("p (k n) -> p k n", k=4)

        block = ctx.enter_context(nc.Block())

        @block.sync
        def _(sp):
            def slot_free(n, layer):
                if n < RAW:
                    pre_free(RAW + n)
                    sp.wait_ge(lo_ready, layer * UNITS + ONE)
                    return
                kind, w = STREAM[n - RAW]
                if kind == "w":
                    sp.wait_ge(lo_ready, layer * UNITS + (ONE + w + 1))
                else:
                    sp.wait_ge(acc_ready if w % 2 else half_ready, layer * 12 + (PRE_BLOCKS + w // 2 + 1))

            def pre_free(a):
                if a < 2:
                    sp.wait_ge(pre_pe, a + 1)
                else:
                    sp.wait_ge(acc_ready if a % 2 else half_ready, a // 2)

            sp.dma_start(c_rows[:, :], c.rearrange("b (k p) -> (b k) p", p=P)).then_inc(c_in, 16)
            sp.dma_start(tab[:, 0:C_STRICT], table[:, 0:C_STRICT]).then_inc(c_in, 16)
            sp.dma_start(b_rows[:, :], b_ada.rearrange("l (k p) -> (l k) p", p=P)).then_inc(small_in, 16)
            for i, v in enumerate((ln1_g, ln1_b, ln2_g, ln2_b)):
                sp.dma_start(ln_rows[DEPTH * KT * i:DEPTH * KT * (i + 1), :],
                             v.rearrange("l (k p) -> (l k) p", p=P)).then_inc(small_in, 16)
            for a in range(PRE_ADA):
                if a >= RAW:
                    pre_free(a - RAW)
                sp.dma_start(wide(a % RAW), ada_v[:, 4 * (a % 2):4 * (a % 2) + 4,
                                                  512 * (a // 2):512 * (a // 2) + 512]).then_inc(raw_in[a % RAW], 16)
            with sp.Fori(0, DEPTH) as l:
                k_d = [sp.snap(l * KT + 4 * i) for i in range(2)]
                k_f = [sp.snap(l * 2 * KT + 4 * i) for i in range(4)]
                for n, (kind, w) in enumerate(STREAM):
                    slot = n % RAW
                    dst = wide(slot)
                    if kind == "ada":
                        chunk, half = w // 4, w % 4
                        col = D * chunk + 512 * (half // 2)
                        k0 = (DEPTH - 1) * KT + 4 * (half % 2)
                        src = ada_v[:, k0:k0 + 4, col:col + 512] if chunk < NEXT_CHUNKS \
                            else ada_v[:, bass.ds(k_d[half % 2], 4), col:col + 512]
                    elif w < U_GATE:
                        col = IN_BLOCKS[w // 2][0]
                        src = in_v[:, bass.ds(k_d[w % 2], 4), col:col + 512]
                    elif w < U_BR:
                        col = GATE0 + 512 * ((w - U_GATE) // 2)
                        src = in_v[:, bass.ds(k_d[w % 2], 4), col:col + 512]
                    elif w < U_O:
                        dst = raw[:, slot, :].rearrange("p (k n) -> p k n", k=8)
                        src = br_v[:, bass.ds(k_d[0], 8), 256 * (w - U_BR):256 * (w - U_BR) + 256]
                    elif w < U_UP:
                        ob, kb = O_ORDER[w - U_O]
                        src = o_v[:, bass.ds(k_d[kb], 4), 512 * ob:512 * ob + 512]
                    elif w < U_DOWN:
                        m = (w - U_UP) // 2
                        col = DFF * (m % 2) + 512 * (m // 2)
                        src = up_v[:, bass.ds(k_d[w % 2], 4), col:col + 512]
                    else:
                        ob, kb = DOWN_ORDER[w - U_DOWN]
                        src = down_v[:, bass.ds(k_f[kb], 4), 512 * ob:512 * ob + 512]
                    slot_free(n, l)
                    sp.sem_inc(seen_sp, 1)
                    sp.dma_start(dst, src).then_inc(raw_in[slot], 16)
            for r in range(RB):
                sp.wait_ge(out_ready, r + 1)
                sp.dma_start(out.rearrange("b (r p) d -> p (b r) d", p=P)[:, r, :], xr[:, r, :]).then_inc(out_done, 16)
            sp.wait_ge(out_done, 16 * RB)

        @block.gpsimd
        def _(pool):
            pool.memset(nhalf[:, :], -0.5).then_inc(nhalf_ready, 1)
            pool.dma_start(xr[:, :, :], x.rearrange("b (r p) d -> p (b r) d", p=P)).then_inc(x_in, 16)
            pool.dma_start(pos_i[:, :], positions.rearrange("b (r p) -> p (b r)", p=P),
                           allow_slow_non_contiguous=True).then_inc(x_in, 16)
            for i, v in enumerate((lam_q1, lam_k1, lam_q2, lam_k2)):
                pool.dma_start(lam_in[:, i, :, :], v.partition_broadcast(P)).then_inc(x_in, 16)
            pool.dma_start(sub_g[:, :, :], subln_g.partition_broadcast(P)).then_inc(x_in, 16)
            pool.dma_start(f_b[:, :, :], forget_b.partition_broadcast(P)).then_inc(x_in, 16)
            pool.dma_start(wf[:, :, :], in_v[:, :, 12 * BW:12 * BW + 4]).then_inc(x_in, 16)
            pool.dma_start(tab[:, C_STRICT:NCONST], table[:, C_STRICT:NCONST]).then_inc(masks_in, 16)
            pool.memset(ln_g[:, :], 1.0).then_inc(plain_ln, 1)
            pool.memset(ln_b[:, :], 0.0).then_inc(plain_ln, 1)
            pool.wait_ge(nhalf_ready, 1)

            def power(layer, k, lo, n):
                pool.wait_ge(var_ready, layer * 5 + (k + 1))
                pool.tensor_tensor(rstd[:, lo:lo + n], ve[:, lo:lo + n], nhalf[:, 0:n], ALU.pow).then_inc(rstd_ready, 1)

            def row(t, layer, lo, n):
                return t[bass.ds(layer, 1), lo:lo + n].rearrange("l n -> (l n)").partition_broadcast(P)

            with pool.Fori(0, DEPTH) as l:
                pool.wait_ge(x_done, l * 4 + 2)
                pool.sem_inc(seen_pool, 1)
                pool.dma_start(cv_rows[0:96, :], conv_w.rearrange("l t (k p) -> (l t k) p", p=P)[
                    bass.ds(l * 96, 96), :]).then_inc(cv_in, 16)
                pool.dma_start(cv_rows[96:128, :], conv_b.rearrange("l (k p) -> (l k) p", p=P)[
                    bass.ds(l * 32, 32), :]).then_inc(cv_in, 16)
                pool.dma_start(g_row[:, :], row(b_ada, l, 2 * D, D)).then_inc(g_in, 16)
                pool.wait_ge(affine_done, l * 2 + 1)
                pool.sem_inc(seen_pool, 1)
                pool.dma_start(ln_g[:, :], row(ln1_g, l, 0, D)).then_inc(ln_in, 16)
                pool.dma_start(ln_b[:, :], row(ln1_b, l, 0, D)).then_inc(ln_in, 16)
                power(l, 0, 0, 8)
                power(l, 1, 0, 1)
                power(l, 2, 1, 1)
                pool.wait_ge(x_done, l * 4 + 4)
                pool.sem_inc(seen_pool, 1)
                pool.dma_start(g_row[:, :], row(b_ada, l, 5 * D, D)).then_inc(g_in, 16)
                pool.wait_ge(affine_done, l * 2 + 2)
                pool.sem_inc(seen_pool, 1)
                pool.dma_start(ln_g[:, :], row(ln2_g, l, 0, D)).then_inc(ln_in, 16)
                pool.dma_start(ln_b[:, :], row(ln2_b, l, 0, D)).then_inc(ln_in, 16)
                power(l, 3, 0, 1)
                power(l, 4, 1, 1)

        @block.scalar
        def _(act):
            own = Own(act, act_own, ACT_OWN)
            act.sem_inc(pt_ready, ONE)

            act.wait_ge(s_full, 1)
            act.activation(sc_tmp[:, 0, :], small[0][:, 0:KT], ACT.Copy).then_inc(pre_act, 1)
            act.activation(sc_tmp[:, 1, :], small[0][:, 0:KT], ACT.Tanh, scale=0.5).then_inc(s_free[0], 1)
            act.wait_ge(s_full, 2)
            act.activation(b_col[:, :], small[1][:, 0:LN_COL + 4 * DEPTH * KT], ACT.Copy).then_inc(s_free[1], 1)
            act.wait_ge(pre_dve, 1)
            act.activation(lam_s[:, :, :], lam_s[:, :, :], ACT.Exp).then_inc(pre_act, 1)
            act.wait_ge(pre_dve, 2)
            act.activation(sin_t[:, :, :], ang[:, :, :], ACT.Sin).then_inc(pre_act, 1)
            act.activation(cos_t[:, :, :], ang_c[:, :, :], ACT.Sin).then_inc(pre_act, 1)

            with act.Fori(0, DEPTH) as l:
                own.enter(l)

                def hi(w):
                    n = AT[("w", w)]
                    s, g = n % RAW, (PRE_ADA + n) // RAW + 1
                    act.wait_ge(raw_in[s], l * (16 * NSTREAM // RAW) + 16 * g)
                    kind, n_done = unit_end(w - SPLIT)
                    act.wait_ge(mm_full if kind else unit_done, l * (NMM if kind else NPLAIN) + (ONE + n_done))
                    act.activation(w_hi[:, w % SPLIT, :], raw[:, s, :], ACT.Copy).then_inc(hi_ready, 1)

                def modulate(which):
                    act.wait_ge(mod_ready, l * 8 + (4 if which == 0 else 12))
                    for j in range(4):
                        k = S_AT[("x", which, j)]
                        act.wait_ge(s_full, l * NSMALL + (PRE_SMALL + k + 1))
                        for t in range(2):
                            ft = 2 * j + t
                            last = act.activation(h_f32[:, ft, :], small[k % 2][:, SEQ * t:SEQ * t + SEQ], ACT.Identity,
                                                  bias=mod[:, 2 * which, ft:ft + 1],
                                                  scale=mod[:, 2 * which + 1, ft:ft + 1])
                            if t == 0:
                                own.mark(last)
                        last.then_inc(s_free[k % 2], 1)
                        own.after(own.n)
                        act.wait_ge(s_free[k % 2], l * (NSMALL // 2) + (PRE_SMALL // 2 + k // 2 + 2))
                        act.activation(h_hi[:, 2 * j:2 * j + 2, :], h_f32[:, 2 * j:2 * j + 2, :],
                                       ACT.Copy).then_inc(h_hi_ready, 1)

                def mm_wait(u, t=0):
                    n = MM_AT[(u, t)]
                    act.wait_ge(mm_full, l * NMM + (ONE + n + 1))
                    return mm[n % 2], mm_free[n % 2]

                def projections(b):
                    bank, free = mm_wait(2 * b + 1)
                    if b == 5:
                        act.wait_ge(s_full, l * NSMALL + (PRE_SMALL + S_AT[("qk", "A", 1)] + 1))
                    where = [(v_a, q_T[0]), (k_T[0], v_b), (v_c, q_T[1]), (k_T[1], v_d)]
                    for half in range(2):
                        src = bank[:, 2 * half:2 * half + 2, :]
                        if b < 4:
                            dst = where[b][half]
                            scale = 0.125 if dst in (q_T[0], q_T[1]) else 1.0
                            ins = act.activation(dst[:, :, :], src, ACT.Copy, scale=scale)
                        else:
                            ins = act.activation(qk_rows[:, :, half, :], src, ACT.Copy)
                        own.mark(ins) if half == 0 else ins.then_inc(free, 1)

                def gate(g):
                    bank, free = mm_wait(U_GATE + 2 * g + 1)
                    act.activation(gates[:, g // 2, 4 * (g % 2):4 * (g % 2) + 4, :], bank[:, :, :], ACT.Tanh,
                                   scale=0.5).then_inc(free, 1)

                def softplus_log(src, dst):
                    own.link(act.activation(dst, src, ACT.Abs))
                    own.link(act.activation(dst, dst, ACT.Exp, scale=-1.0))
                    act.activation(dst, dst, ACT.Ln, bias=1.0).then_inc(log_ready, 1)

                def head_first(i):
                    b, h = HEADS[i]
                    if b == "B":
                        act.wait_ge(z_ready, l * 4 + (h + 1))
                        softplus_log(probs[:, prob_slot(i, 0), :], soft[:, h % 2, :])
                        return
                    for j in range(2 if b == "A" else 1):
                        k = K_AT[(i, j)]
                        act.wait_ge(sm_ready, l * 16 + (k - 4 + 1))
                        pr = probs[:, prob_slot(i, j), :]
                        act.activation(pr[:, 0:P], pr[:, 0:P], ACT.Exp, bias=nmax[:, k, 0:1],
                                       accum_out=den[:, k, 0:1]).then_inc(exp_ready, 1)
                        act.activation(pr[:, P:3 * P], pr[:, P:3 * P], ACT.Exp, bias=nmax[:, k, 1:2],
                                       accum_out=den[:, k, 1:2]).then_inc(exp_ready, 1)

                def head_second(i):
                    b, h = HEADS[i]
                    if b == "B":
                        act.wait_ge(la_ready, l * 4 + (h + 1))
                        pr = probs[:, prob_slot(i, 0), :]
                        act.activation(pr, pr, ACT.Exp).then_inc(exp_ready, 1)

                def probs_T(i):
                    act.wait_ge(tr_full, l * NTR + (TR.index(("p", i)) + 1))
                    if i >= 2:
                        act.wait_ge(pv_done, l * 16 + (i - 1))
                    act.activation(p_T[:, i % 2, :], turn[:, 0:384], ACT.Copy).then_inc(pt_ready, 1)

                def qk_T(b, j):
                    s = 0 if b == "A" else 1
                    k = S_AT[("qk", b, j)]
                    act.wait_ge(s_full, l * NSMALL + (PRE_SMALL + k + 1))
                    dst = (q_T if j == 0 else k_T)[s]
                    act.activation(dst[:, :, :], small[k % 2][:, :].rearrange("p (t q) -> p t q", t=2), ACT.Copy,
                                   scale=0.125 if (b, j) == ("C", 0) else 1.0).then_inc(s_free[k % 2], 1)

                def branch_hi(o):
                    k = S_AT[("o", o, 0)]
                    n = "ABCD".index(ORDER[o])
                    act.wait_ge(s_full, l * NSMALL + (PRE_SMALL + k + 1))
                    act.activation(br_hi[:, 2 * n:2 * n + 2, :], small[k % 2][:, :].rearrange("p (t q) -> p t q", t=2),
                                   ACT.Copy).then_inc(br_hi_ready, 1)

                def merged_hi(dt):
                    act.wait_ge(merged_ready, l * KT + (dt + 1))
                    act.activation(h_hi[:, dt, :], gated[:, dt % 2, 0, :], ACT.Copy, scale=0.5).then_inc(m_hi_ready, 1)

                def conv_base(m):
                    bank, _ = mm_wait(U_UP + 2 * m + 1)
                    if m >= 2:
                        act.wait_ge(act_lo_ready, l * 4 + m // 2)
                    y = (y_a, y_g)[m % 2]
                    for t in range(4):
                        f = 16 * (m % 2) + 4 * (m // 2) + t
                        act.activation(y[:, t, :], bank[:, t, :], ACT.Identity, bias=cv[:, 96 + f:97 + f],
                                       scale=cv[:, 64 + f:65 + f]).then_inc(base_ready, 1)

                def ffn_tanh(j):
                    act.wait_ge(conv_ready, l * 4 + (j + 1))
                    act.activation(th[:, :, :], y_a[:, :, :], ACT.Tanh, scale=0.5).then_inc(tanh_ready, 1)

                def ffn_hi(j):
                    act.wait_ge(prod_ready, l * 4 + (j + 1))
                    act.activation(act_hi[:, 4 * j:4 * j + 4, :], y_g[:, :, :], ACT.Copy).then_inc(act_hi_ready, 1)

                hi(0)
                hi(1)
                hi(2)
                modulate(0)
                hi(3)
                act.wait_ge(tr_full, l * NTR + 1)
                act.activation(cv[:, :], turn[:, 0:P], ACT.Copy).then_inc(tr_free, 1)

                for s in range(2, UNITS + 1):
                    if U_UP + 3 <= s <= U_DOWN + 1 and s % 2:
                        m = (s - U_UP - 3) // 2
                        (ffn_hi if m % 2 else ffn_tanh)(m // 2)
                    if s % 2 == 0 and 14 <= s <= 28:
                        gate(s // 2 - 7)
                    if s + 2 < UNITS:
                        hi(s + 2)
                    if s - 1 in QK_AFTER:
                        qk_T(*QK_AFTER[s - 1])
                    if s in (2, 4, 6, 8, 10, 13):
                        projections((s - 2) // 2)
                    if s == 2:
                        act.wait_ge(f_ready, l + 1)
                        softplus_log(f_v[:, :, :], f_l[:, :, :])
                    if 0 <= s - 9 < 16:
                        probs_T(s - 9)
                    if 0 <= s - 7 < 16:
                        head_second(s - 7)
                    if 0 <= s - 6 < 16:
                        head_first(s - 6)
                    if s - 1 in OT_AFTER:
                        branch_hi(OT_AFTER[s - 1])
                    if U_BR < s <= U_BR + 4:
                        merged_hi(2 * (s - U_BR) - 1)
                    if U_BR <= s < U_BR + 4:
                        merged_hi(2 * (s - U_BR))
                    if s == U_UP:
                        modulate(1)
                    if U_UP + 2 <= s <= U_DOWN and s % 2 == 0:
                        m = (s - U_UP) // 2 - 1
                        conv_base(m)
                own.leave()

        @block.vector
        def _(dve):
            own = Own(dve, dve_own, DVE_OWN)
            dve.sem_inc(lo_ready, ONE)
            own.link(dve.memset(ones[:, :], 1.0))

            def ada_unit(slot, half, buf):
                for k in range(4):
                    wk = wide(slot)[:, k, :]
                    sc = sc_col[:, 4 * half + k:4 * half + k + 1]
                    if half == 0 and k == 0:
                        ins = dve.tensor_scalar(acc[:, buf, :], wk, sc, None, ALU.mult)
                    else:
                        ins = dve.scalar_tensor_tensor(out=acc[:, buf, :], in0=wk, scalar=sc, in1=acc[:, buf, :],
                                                       op0=ALU.mult, op1=ALU.add)
                    if k < 3:
                        own.link(ins)
                    else:
                        ins.then_inc(acc_ready if half else half_ready, 1)

            def column(k, row, half, bias):
                src = small[k % 2][:, 0:4]
                dst = mod[:, row, 4 * half:4 * half + 4]
                if row % 2:
                    return dve.scalar_tensor_tensor(out=dst, in0=src, scalar=1.0, in1=bias, op0=ALU.add, op1=ALU.add)
                return dve.tensor_tensor(dst, src, bias, ALU.add)

            dve.wait_ge(pre_act, 1)
            dve.wait_ge(s_free[0], 2)
            own.link(dve.tensor_scalar(sc_tmp[:, 1, :], sc_tmp[:, 1, :], 0.5, 0.5, ALU.mult, ALU.add))
            own.link(dve.tensor_tensor(sc_col[:, :], sc_tmp[:, 0, :], sc_tmp[:, 1, :], ALU.mult))
            dve.sem_inc(sc_ready, 1)

            def pre_block(blk):
                for half in range(2):
                    a = 2 * blk + half
                    if a == 6:
                        dve.wait_ge(s_full, 4)
                    dve.wait_ge(raw_in[a % RAW], 16 * (a // RAW + 1))
                    if half:
                        dve.wait_ge(half_ready, blk)
                    ada_unit(a % RAW, half, (blk - 1) % 2)

            pre_block(1)
            dve.wait_ge(x_in, 16 * 9)
            dve.wait_ge(c_in, 32)
            for i in range(2):
                own.link(dve.tensor_tensor(lam_in[:, 2 * i, :, :], lam_in[:, 2 * i, :, :], lam_in[:, 2 * i + 1, :, :],
                                           ALU.mult))
                ins = dve.tensor_reduce(lam_s[:, i, :], lam_in[:, 2 * i, :, :], AX_X, ALU.add)
                own.link(ins)
            dve.sem_inc(pre_dve, 1)
            own.link(dve.tensor_copy(pos_f[:, :], pos_i[:, :]))
            for r in range(RB):
                ins = dve.tensor_scalar(ang[:, r, :], tab[:, C_FREQ:C_FREQ + CA + CC], pos_f[:, r:r + 1], None, ALU.mult)
            own.link(ins)
            big = 1.5 * 2.0 ** 23
            own.link(dve.tensor_scalar(ang_k[:, :, :], ang[:, :, :], 1.0 / (2.0 * math.pi), big, ALU.mult, ALU.add))
            own.link(dve.tensor_scalar(ang_k[:, :, :], ang_k[:, :, :], big, None, ALU.subtract))
            rest = 2.0 * math.pi
            for bits in (5, 13, 21, 60):
                part = rest if bits == 60 else math.floor(rest * 2.0 ** bits) / 2.0 ** bits
                rest -= part
                own.link(dve.scalar_tensor_tensor(out=ang[:, :, :], in0=ang_k[:, :, :], scalar=-part, in1=ang[:, :, :],
                                                  op0=ALU.mult, op1=ALU.add))
            pi = 3.1415925
            own.link(dve.tensor_scalar(ang[:, :, :], ang[:, :, :], pi, -pi, ALU.min, ALU.max))
            own.link(dve.tensor_scalar(ang_c[:, :, :], ang[:, :, :], math.pi / 2, None, ALU.add))
            own.link(dve.tensor_scalar(ang_k[:, :, :], ang_c[:, :, :], math.pi, -2.0 * math.pi, ALU.is_gt, ALU.mult))
            own.link(dve.tensor_tensor(ang_c[:, :, :], ang_c[:, :, :], ang_k[:, :, :], ALU.add))
            dve.tensor_scalar(ang_c[:, :, :], ang_c[:, :, :], pi, -pi, ALU.min, ALU.max).then_inc(pre_dve, 1)
            dve.wait_ge(pre_act, 2)
            own.link(dve.tensor_tensor(lam_n[:, :], lam_s[:, 1, :], lam_s[:, 0, :], ALU.subtract))
            own.link(dve.tensor_tensor(lam_n[:, :], lam_n[:, :], tab[:, C_LI:C_LI + DEPTH], ALU.subtract))
            for l0 in range(DEPTH):
                own.link(dve.tensor_scalar(sub_g[:, l0, :], sub_g[:, l0, :], tab[:, C_LI + DEPTH + l0:C_LI + DEPTH + l0 + 1],
                                           None, ALU.mult))
            dve.wait_ge(s_free[1], 2)
            for k in range(4):
                if k < 2:
                    pre_block(k + 2)
                dve.wait_ge(s_full, 2 + k + 1)
                column(k, k // 2, k % 2, b_col[:, 4 * k:4 * k + 4]).then_inc(s_free[k % 2], 1)
            dve.wait_ge(s_free[0], 4)
            dve.wait_ge(s_free[1], 4)
            dve.sem_inc(mod_ready, 4)
            dve.sem_inc(x_done, RB)
            dve.wait_ge(plain_ln, 2)
            dve.wait_ge(pre_act, 4)

            with dve.Fori(0, DEPTH) as l:
                own.enter(l)

                def lo(w):
                    n = AT[("w", w)]
                    dve.wait_ge(hi_ready, l * UNITS + (w + 1))
                    dve.tensor_tensor(w_lo[:, w % SPLIT, :], raw[:, n % RAW, :], w_hi[:, w % SPLIT, :].bitcast(F32),
                                      ALU.subtract).then_inc(lo_ready, 1)

                def ada(a):
                    n = AT[("ada", a)]
                    blk = a // 2
                    dve.wait_ge(raw_in[n % RAW], l * (16 * NSTREAM // RAW) + 16 * ((PRE_ADA + n) // RAW + 1))
                    if a % 2 == 0 and blk >= 2:
                        dve.wait_ge(s_full, l * NSMALL + (PRE_SMALL + S_AT[("ada", blk - 2, 0)] + 1))
                    if a % 2:
                        dve.wait_ge(half_ready, l * 12 + (PRE_BLOCKS + blk + 1))
                    ada_unit(n % RAW, a % 2, blk % 2)

                def s_wait(key):
                    k = S_AT[key]
                    dve.wait_ge(s_full, l * NSMALL + (PRE_SMALL + k + 1))
                    return small[k % 2], s_free[k % 2]

                def ada_out(blk):
                    bank, free = s_wait(("ada", blk, 0))
                    chunk, half = blk // 2, blk % 2
                    if chunk in GATE_CHUNKS:
                        if half == 0:
                            dve.wait_ge(g_in, l * 32 + (16 if chunk == GATE_CHUNKS[0] else 32))
                        g = g_row[:, 512 * half:512 * half + 512]
                        dve.tensor_tensor(g, bank[:, :], g, ALU.add).then_inc(free, 1)
                        return
                    if chunk < NEXT_CHUNKS:
                        dst_row = chunk
                        b0 = (DEPTH - 1) * 48 + 8 * chunk + 4 * half
                        bias = b_col[:, b0:b0 + 4]
                    else:
                        dst_row = chunk - 1
                        bias = b_col[:, bass.ds(l * 48 + (8 * chunk + 4 * half), 4)]
                    own.link(column(S_AT[("ada", blk, 0)], dst_row, half, bias))
                    if dst_row % 2:
                        cols = slice(4 * half, 4 * half + 4)
                        scale, shift = mod[:, dst_row, cols], mod[:, dst_row - 1, cols]
                        g, b = (b_col[:, bass.ds(l * KT + (LN_COL + DEPTH * KT * (i + (2 if dst_row == 1 else 0))
                                                           + 4 * half), 4)] for i in range(2))
                        own.link(dve.tensor_tensor(mod_t[:, :], scale, b, ALU.mult))
                        own.link(dve.tensor_tensor(shift, shift, mod_t[:, :], ALU.add))
                        own.link(dve.tensor_tensor(scale, scale, g, ALU.mult))
                    dve.sem_inc(free, 1)
                    dve.sem_inc(mod_ready, 1)

                def h_low(which):
                    for j in range(4):
                        dve.wait_ge(h_hi_ready, l * 8 + (4 * which + j + 1))
                        dve.tensor_tensor(h_lo[:, 2 * j:2 * j + 2, :], h_f32[:, 2 * j:2 * j + 2, :],
                                          h_hi[:, 2 * j:2 * j + 2, :].bitcast(F32), ALU.subtract)\
                            .then_inc(h_lo_ready, 1)

                def forget_logits():
                    dve.wait_ge(tr_full, l * NTR + 2)
                    dve.tensor_tensor(f_v[:, :, :], turn[:, 0:8].rearrange("p (r h) -> p r h", r=RB),
                                      fb_cur[:, :].unsqueeze(1).broadcast_to([P, RB, 4]), ALU.add).then_inc(f_ready, 1)
                    dve.wait_ge(f_ready, l + 1)
                    dve.sem_inc(tr_free, 1)

                def log_forget():
                    dve.wait_ge(log_ready, l * 5 + 1)
                    own.link(dve.scalar_tensor_tensor(out=f_lf[:, :, :], in0=f_v[:, :, :], scalar=0.0, in1=f_l[:, :, :],
                                                      op0=ALU.min, op1=ALU.subtract))
                    dve.tensor_copy(lf_b[:, :, :], f_lf[:, :, :].rearrange("p r h -> p (r h)").unsqueeze(2)
                                    .broadcast_to([P, 8, P])).then_inc(lf_ready, 1)

                def slot_wait(i, j):
                    if j == 0 and i >= 4:
                        dve.wait_ge(tr_full, l * NTR + (TR.index(("p", i - 4)) + 1))

                def head_first(i):
                    b, h = HEADS[i]
                    if i == 0:
                        dve.wait_ge(masks_in, 16)
                    for j in range(2 if b == "A" else 1):
                        k = K_AT[(i, j)]
                        bank, free = s_wait(("s", i, j))
                        slot_wait(i, j)
                        pr = probs[:, prob_slot(i, j), :]
                        if b == "B":
                            own.link(dve.tensor_tensor(pr, bank[:, 0:384], tab[:, C_STRICT:C_STRICT + 384], ALU.add))
                            dve.sem_inc(z_ready, 1)
                            dve.sem_inc(free, 1)
                            continue
                        m0 = C_DIL if b == "C" else C_CAUSAL
                        scale = 32.0 ** -0.5 if b == "A" else 1.0
                        dve.sem_inc(seen_dve, 1)
                        own.mark(dve.tensor_tensor_reduce(
                            pr[:, 0:P], bank[:, 0:P], tab[:, m0:m0 + P], scale, -3e38, ALU.add, ALU.max,
                            tmax[:, k, 0:1]))
                        a2 = own.mark(dve.tensor_tensor_reduce(
                            pr[:, P:3 * P], bank[:, P:3 * P], tab[:, m0 + P:m0 + 3 * P], scale, -3e38, ALU.add,
                            ALU.max, tmax[:, k, 1:2]))
                        own.after(a2)
                        dve.sem_inc(free, 1)
                        dve.tensor_scalar(nmax[:, k, :], tmax[:, k, :], -1.0, None, ALU.mult).then_inc(sm_ready, 1)

                def exp_count(i):
                    return sum({"B": 1, "D": 2, "A": 4, "C": 2}[HEADS[n][0]] for n in range(i + 1))

                def head_second(i):
                    b, h = HEADS[i]
                    if b == "B":
                        pr, sp_ = probs[:, prob_slot(i, 0), :], soft[:, h % 2, :]
                        dve.wait_ge(log_ready, l * 5 + (1 + h + 1))
                        own.link(dve.scalar_tensor_tensor(out=sp_, in0=pr, scalar=0.0, in1=sp_, op0=ALU.max, op1=ALU.add))
                        dve.tensor_tensor_scan(sp_[:, 0:P][:, ::-1], ones[:, 0:P], sp_[:, 0:P][:, ::-1], 0.0,
                                               ALU.mult, ALU.add)
                        own.link(dve.tensor_tensor_scan(sp_[:, P:3 * P][:, ::-1], ones[:, 0:2 * P],
                                                        sp_[:, P:3 * P][:, ::-1], 0.0, ALU.mult, ALU.add))
                        dve.tensor_tensor(pr, pr, sp_, ALU.subtract).then_inc(la_ready, 1)
                        return
                    dve.wait_ge(exp_ready, l * 36 + exp_count(i))
                    if b != "A":
                        o = ORDER.index(b)
                        own.link(dve.reciprocal(rden[:, o, :, h], den[:, K_AT[(i, 0)], :]))
                        return
                    k0, k1 = K_AT[(i, 0)], K_AT[(i, 1)]
                    p0, p1 = probs[:, prob_slot(i, 0), :], probs[:, prob_slot(i, 1), :]
                    dve.reciprocal(rsub[:, h, 0, :], den[:, k0, :])
                    own.link(dve.reciprocal(rsub[:, h, 1, :], den[:, k1, :]))
                    own.link(dve.tensor_scalar(rsub[:, h, 1, :], rsub[:, h, 1, :], lam_cur[:, 0:1], None, ALU.mult))
                    dve.tensor_scalar(p1[:, 0:P], p1[:, 0:P], rsub[:, h, 1, 0:1], None, ALU.mult)
                    own.link(dve.tensor_scalar(p1[:, P:3 * P], p1[:, P:3 * P], rsub[:, h, 1, 1:2], None, ALU.mult))
                    dve.scalar_tensor_tensor(out=p0[:, 0:P], in0=p0[:, 0:P], scalar=rsub[:, h, 0, 0:1], in1=p1[:, 0:P],
                                             op0=ALU.mult, op1=ALU.add)
                    dve.scalar_tensor_tensor(out=p0[:, P:3 * P], in0=p0[:, P:3 * P], scalar=rsub[:, h, 0, 1:2],
                                             in1=p1[:, P:3 * P], op0=ALU.mult, op1=ALU.add).then_inc(mix_ready, 1)

                def rope(b):
                    n, r0, half = (16, 0, CA) if b == "A" else (8, CA, CC)
                    dve.wait_ge(mm_free[0 if b == "A" else 1], l * (NMM // 2) + (1 + 3))
                    v = qk_rows[:, :, :, :].rearrange("p r c (h d) -> p r (c h) d", d=BW * 2 // n)
                    x1, x2 = v[:, :, :, 0:half], v[:, :, :, half:2 * half]
                    cos = cos_t[:, :, r0:r0 + half].unsqueeze(2).broadcast_to([P, RB, n, half])
                    sin = sin_t[:, :, r0:r0 + half].unsqueeze(2).broadcast_to([P, RB, n, half])
                    t = [rot[:, i, :].rearrange("p (r h d) -> p r h d", r=RB, h=n) for i in range(4)]
                    dve.tensor_tensor(t[0], x1, cos, ALU.mult)
                    dve.tensor_tensor(t[1], x2, sin, ALU.mult)
                    dve.tensor_tensor(t[2], x2, cos, ALU.mult)
                    own.link(dve.tensor_tensor(t[3], x1, sin, ALU.mult))
                    dve.tensor_tensor(x1, t[0], t[1], ALU.subtract)
                    dve.tensor_tensor(x2, t[2], t[3], ALU.add).then_inc(rope_ready, 1)

                def branch_rows(o):
                    b = ORDER[o]
                    dve.wait_ge(ov_full, l * 4 + (o + 1))
                    if o >= 1:
                        dve.wait_ge(s_full, l * NSMALL + (PRE_SMALL + S_AT[("o", o - 1, 0)] + 1))
                    src = ov[:, :].rearrange("p (r h d) -> p r h d", r=RB, h=4)
                    if b in "CD":
                        ins = dve.tensor_tensor(o_rows[:, :, :, :], src,
                                                rden[:, o, :, :].unsqueeze(3).broadcast_to([P, RB, 4, HD]), ALU.mult)
                    else:
                        ins = dve.tensor_copy(o_rows[:, :, :, :], src)
                    own.link(ins)
                    dve.sem_inc(ov_free, 1)
                    if b == "A":
                        own.link(dve.tensor_tensor(o_sq[:, :, :, :], o_rows[:, :, :, :], o_rows[:, :, :, :], ALU.mult))
                        own.link(dve.tensor_reduce(ve[:, 0:8].rearrange("p (r h) -> p r h", r=RB), o_sq[:, :, :, :],
                                                   AX_X, ALU.add))
                        own.link(dve.tensor_scalar(ve[:, 0:8], ve[:, 0:8], 1.0 / HD, EPS, ALU.mult, ALU.add))
                        dve.sem_inc(var_ready, 1)
                        dve.wait_ge(rstd_ready, l * 5 + 1)
                        own.link(dve.tensor_tensor(
                            o_rows[:, :, :, :], o_rows[:, :, :, :],
                            rstd[:, 0:8].rearrange("p (r h) -> p r h", r=RB).unsqueeze(3).broadcast_to([P, RB, 4, HD]),
                            ALU.mult))
                        own.link(dve.tensor_tensor(
                            o_rows[:, :, :, :].rearrange("p r h d -> p (r h) d"),
                            o_rows[:, :, :, :].rearrange("p r h d -> p (r h) d"),
                            sub_cur[:, :].unsqueeze(1).broadcast_to([P, 8, HD]), ALU.mult))
                    dve.sem_inc(o_ready, 1)

                def branch_lo(o):
                    bank, free = s_wait(("o", o, 0))
                    n = "ABCD".index(ORDER[o])
                    dve.wait_ge(br_hi_ready, l * 4 + (o + 1))
                    dve.tensor_tensor(br_lo[:, 2 * n:2 * n + 2, :], bank[:, :].rearrange("p (t q) -> p t q", t=2),
                                      br_hi[:, 2 * n:2 * n + 2, :].bitcast(F32), ALU.subtract).then_inc(br_lo_ready, 1)
                    dve.wait_ge(br_lo_ready, l * 4 + (o + 1))
                    dve.sem_inc(free, 1)

                def merge(dt):
                    n = MM_AT[(U_BR + dt // 2, dt % 2)]
                    dve.wait_ge(mm_full, l * NMM + (ONE + n + 1))
                    g = gated[:, dt % 2, :, :]
                    if dt >= 2:
                        dve.wait_ge(m_lo_ready, l * KT + (dt - 1))
                    own.link(dve.scalar_tensor_tensor(out=g, in0=gates[:, :, dt, :], scalar=1.0, in1=mm[n % 2][:, :, :],
                                                      op0=ALU.add, op1=ALU.mult))
                    dve.sem_inc(mm_free[n % 2], 1)
                    own.link(dve.tensor_tensor(g[:, 0:2, :], g[:, 0:2, :], g[:, 2:4, :], ALU.add))
                    dve.tensor_tensor(g[:, 0, :], g[:, 0, :], g[:, 1, :], ALU.add).then_inc(merged_ready, 1)

                def merged_lo(dt):
                    dve.wait_ge(m_hi_ready, l * KT + (dt + 1))
                    dve.scalar_tensor_tensor(out=h_lo[:, dt, :], in0=gated[:, dt % 2, 0, :], scalar=0.5,
                                             in1=h_hi[:, dt, :].bitcast(F32), op0=ALU.mult, op1=ALU.subtract)\
                        .then_inc(m_lo_ready, 1)

                def residual(which, ob, r):
                    u = (U_O + 2, U_DOWN + 6)[which] + ob
                    n = MM_AT[(u, 0)]
                    if r == 0:
                        dve.wait_ge(row0_full, l * 4 + (2 * which + ob + 1))
                    else:
                        dve.wait_ge(mm_full, l * NMM + (ONE + n + 1))
                    bank = mm[n % 2][:, :, :].rearrange("p (r a) q -> p r (a q)", r=RB)[:, r, :]
                    t = gated[:, 0, :, :].rearrange("p (r a) q -> p r (a q)", r=RB)[:, r, :]
                    xs = xr[:, r, 512 * ob:512 * ob + 512]
                    dve.wait_ge(m_lo_ready, l * KT + KT)
                    own.link(dve.tensor_tensor(t, bank, g_row[:, 512 * ob:512 * ob + 512], ALU.mult))
                    if r == RB - 1:
                        dve.sem_inc(mm_free[n % 2], 1)
                    own.link(dve.scalar_tensor_tensor(out=xs, in0=xs, scalar=ALPHA, in1=t, op0=ALU.mult, op1=ALU.add))
                    own.link(dve.bn_stats(stats[:, r, ob, :], xs))

                def variance(which, r):
                    dve.sem_inc(seen_dve, 1)
                    own.link(dve.bn_aggr(mv[:, r, :], stats[:, r, :, :].rearrange("p a b -> p (a b)")))
                    dve.tensor_scalar(ve[:, r:r + 1], mv[:, r, 1:2], EPS, None, ALU.add).then_inc(var_ready, 1)

                def normalise(which, r):
                    dve.wait_ge(rstd_ready, l * 5 + (2 * which + r + 2))
                    dve.tensor_scalar(xr[:, r, :], xr[:, r, :], mv[:, r, 0:1], rstd[:, r:r + 1],
                                      ALU.subtract, ALU.mult).then_inc(x_done, 1)

                def affine(which, part):
                    if part == 0:
                        dve.wait_ge(x_done, l * 4 + (2 * which + 2))
                    if (which, part) == (1, 0):
                        dve.wait_ge(ln_in, l * 64 + 32)
                    t, op = ((ln_g, ALU.mult), (ln_b, ALU.add))[part]
                    own.link(dve.tensor_tensor(xr[:, :, :], xr[:, :, :],
                                               t[:, :].unsqueeze(1).broadcast_to([P, RB, D]), op))
                    if part == 1:
                        dve.sem_inc(affine_done, 1)

                def conv_taps(m):
                    n = MM_AT[(U_UP + 2 * m + 1, 0)]
                    bank, y = mm[n % 2], (y_a, y_g)[m % 2]
                    dve.wait_ge(base_ready, l * 32 + 4 * (m + 1))
                    for tap in (1, 0):
                        shift = 2 - tap
                        for t in range(4):
                            f = 16 * (m % 2) + 4 * (m // 2) + t
                            ins = dve.scalar_tensor_tensor(
                                out=y[:, t, shift:SEQ], in0=bank[:, t, 0:SEQ - shift],
                                scalar=cv[:, 32 * tap + f:32 * tap + f + 1], in1=y[:, t, shift:SEQ],
                                op0=ALU.mult, op1=ALU.add)
                        own.link(ins)
                    dve.sem_inc(mm_free[n % 2], 1)

                def ffn_a(j):
                    dve.wait_ge(tanh_ready, l * 4 + (j + 1))
                    own.link(dve.scalar_tensor_tensor(out=y_a[:, :, :], in0=th[:, :, :], scalar=1.0, in1=y_a[:, :, :],
                                                      op0=ALU.add, op1=ALU.mult))

                def ffn_product():
                    dve.scalar_tensor_tensor(out=y_g[:, :, :], in0=y_a[:, :, :], scalar=0.5, in1=y_g[:, :, :],
                                             op0=ALU.mult, op1=ALU.mult).then_inc(prod_ready, 1)

                def ffn_lo(j):
                    dve.wait_ge(act_hi_ready, l * 4 + (j + 1))
                    dve.tensor_tensor(act_lo[:, 4 * j:4 * j + 4, :], y_g[:, :, :],
                                      act_hi[:, 4 * j:4 * j + 4, :].bitcast(F32), ALU.subtract)\
                        .then_inc(act_lo_ready, 1)

                lo(0)
                own.link(dve.tensor_copy(wf_hi[:, :, :], wf[:, bass.ds(l * KT, KT), :]))
                dve.tensor_tensor(wf_lo[:, :, :], wf[:, bass.ds(l * KT, KT), :], wf_hi[:, :, :].bitcast(F32),
                                  ALU.subtract).then_inc(wf_ready, 1)
                dve.tensor_copy(lam_cur[:, :], lam_n[:, bass.ds(l, 1)])
                dve.tensor_copy(sub_cur[:, :].unsqueeze(1), sub_g[:, bass.ds(l, 1), :])
                own.link(dve.tensor_copy(fb_cur[:, :].unsqueeze(1), f_b[:, bass.ds(l, 1), :]))
                h_low(0)
                lo(1)
                lo(2)

                for s in range(2, UNITS + 1):
                    dt = 2 * (s - U_BR)
                    if U_BR < s <= U_BR + 4:
                        merge(dt - 1)
                        merged_lo(dt - 2)
                    if s + 1 < UNITS and s != U_UP:
                        lo(s + 1)
                    if U_BR < s <= U_BR + 4:
                        merged_lo(dt - 1)
                    if U_BR <= s < U_BR + 4:
                        merge(dt)
                    if U_UP + 3 <= s <= U_DOWN + 1 and s % 2:
                        m = (s - U_UP - 3) // 2
                        (ffn_lo if m % 2 else ffn_a)(m // 2)
                    if s == 2:
                        forget_logits()
                    if s == 3:
                        log_forget()
                    if 0 <= s - 7 < 16:
                        head_second(s - 7)
                    if 0 <= s - 6 < 16:
                        head_first(s - 6)
                    if s in (10, 14):
                        rope("A" if s == 10 else "C")
                    if s in (13, 17, 21, 25):
                        branch_rows((s - 13) // 4)
                    if s - 1 in OT_AFTER:
                        branch_lo(OT_AFTER[s - 1])
                    if s in ADA_STEPS:
                        ada(ADA_STEPS.index(s))
                    if s - 1 in ADA_AFTER:
                        ada_out(ADA_AFTER[s - 1])
                    if s in (7, 9):
                        affine(0, (s - 7) // 2)
                    if s in (U_DOWN + 4, U_DOWN + 5):
                        affine(1, s - U_DOWN - 4)
                    for which, first in ((0, U_O + 3), (1, U_DOWN + 7)):
                        for r in range(RB):
                            if s == first:
                                residual(which, 0, r)
                            if s == first + 1:
                                residual(which, 1, r)
                                variance(which, r)
                        for r in range(RB):
                            if s == first + 1:
                                normalise(which, r)
                    if s == U_UP:
                        lo(s + 1)
                        h_low(1)
                    if U_UP + 2 <= s <= U_DOWN and s % 2 == 0:
                        m = (s - U_UP) // 2 - 1
                        conv_taps(m)
                        if m % 2:
                            ffn_product()
                        else:
                            dve.sem_inc(conv_ready, 1)
                dve.wait_ge(ln_in, l * 64 + 64)
                dve.sem_inc(seen_dve, 1)
                own.leave()

            dve.wait_ge(x_done, RB + 4 * DEPTH)
            for r in range(RB):
                dve.tensor_tensor(xr[:, r, :], xr[:, r, :], ln_g[:, :], ALU.mult).then_inc(last_done, 1)
                dve.wait_ge(last_done, r + 1)
                dve.tensor_tensor(xr[:, r, :], xr[:, r, :], ln_b[:, :], ALU.add).then_inc(out_ready, 1)

        @block.tensor
        def _(pe):
            for s in (*mm_free, *s_free, ov_free):
                pe.sem_inc(s, 1)
            for s in (mm_full, unit_done):
                pe.sem_inc(s, ONE)
            pe.wait_ge(c_in, 32)
            pe.wait_ge(s_free[0], 1)
            pe.transpose(small[0][:, 0:8], c_rows[:, :], idn[0:8, 0:8]).then_inc(s_full, 1)
            pe.wait_ge(small_in, 16 * 5)
            pe.wait_ge(s_free[1], 1)
            pe.transpose(small[1][:, 0:LN_COL], b_rows[:, :], idn[0:LN_COL, 0:LN_COL])
            pe.transpose(small[1][:, LN_COL:LN_COL + 4 * DEPTH * KT], ln_rows[:, :],
                         idn[0:4 * DEPTH * KT, 0:4 * DEPTH * KT]).then_inc(s_full, 1)

            def ada_columns(bank, buf):
                for t in range(4):
                    ins = pe.matmul(bank[:, t:t + 1], acc[:, buf, P * t:P * t + P], ones[:, 0:1], start=True, stop=True)
                ins.then_inc(s_full, 1)

            pe.wait_ge(sc_ready, 1)
            pe.wait_ge(s_free[0], 2)
            for half in range(2):
                pe.wait_ge(raw_in[half], 16)
                for t in range(4):
                    for k in range(4):
                        ins = pe.matmul(small[0][:, t:t + 1], wide(half)[:, k, P * t:P * t + P],
                                        sc_col[:, 4 * half + k:4 * half + k + 1],
                                        start=(half, t, k) == (0, 0, 0), stop=(half, k) == (1, 3),
                                        skip_group_check=True)
                ins.then_inc(pre_pe, 1)
            pe.wait_ge(pre_pe, 2)
            pe.sem_inc(s_full, 1)
            for blk in range(1, 4):
                pe.wait_ge(s_free[blk % 2], blk // 2 + 2)
                pe.wait_ge(acc_ready, blk)
                ada_columns(small[blk % 2], (blk - 1) % 2)
            pe.wait_ge(x_in, 16 * 9)

            with pe.Fori(0, DEPTH) as l:
                def s_take(key):
                    k = S_AT[key]
                    pe.wait_ge(s_free[k % 2], l * (NSMALL // 2) + (PRE_SMALL // 2 + k // 2 + 1))
                    return small[k % 2]

                def turn_x(which):
                    for j in range(4):
                        bank = s_take(("x", which, j))
                        for r in range(RB):
                            pe.wait_ge(x_done, l * 4 + (2 * which + r + 1))
                            for t in range(2):
                                ft = 2 * j + t
                                ins = pe.transpose(bank[:, SEQ * t + P * r:SEQ * t + P * r + P],
                                                   xr[:, r, P * ft:P * ft + P], idn)
                        ins.then_inc(s_full, 1)

                def mm_take(n):
                    pe.wait_ge(mm_free[n % 2], l * (NMM // 2) + (n // 2 + 1))
                    return mm[n % 2]

                def passes(out, stat, mov, first, last):
                    pairs = ((stat[0], mov[0]), (stat[0], mov[1]), (stat[1], mov[0]))
                    for i, (a, b) in enumerate(pairs):
                        ins = pe.matmul(out, a, b, start=first and i == 0, stop=last and i == 2,
                                        skip_group_check=True)
                    return ins

                def take_unit(w):
                    pe.wait_ge(hi_ready, l * UNITS + (w + 1))
                    pe.wait_ge(lo_ready, l * UNITS + (ONE + w + 1))
                    return w % SPLIT

                def features_or_rows(w, group, form, src, kh):
                    s = take_unit(w)
                    bank = mm_take(group) if kh == 0 else mm[group % 2]
                    hi, lo = (t[:, s, :].rearrange("p (k n) -> p k n", k=4) for t in (w_hi, w_lo))
                    for half in range(2):
                        for t in range(2):
                            for kk in range(4):
                                k = 4 * kh + kk
                                c0 = 256 * half
                                if form[half] == "T":
                                    sl = slice(c0 + P * t, c0 + P * t + P)
                                    st = (hi[:, kk, sl], lo[:, kk, sl])
                                    mv_ = (src[0][:, k, :], src[1][:, k, :])
                                else:
                                    st = tuple(a[:, k, P * t:P * t + P] for a in src)
                                    mv_ = (hi[:, kk, c0:c0 + 256], lo[:, kk, c0:c0 + 256])
                                ins = passes(bank[:, 2 * half + t, :], st, mv_, first=(k == 0 and t == 0), last=(k == 7))
                    ins.then_inc(mm_full if kh == 1 else unit_done, 1)

                def rows(w, group, src, k0, first, last):
                    s = take_unit(w)
                    bank = mm_take(group) if first else mm[group % 2]
                    out = bank[:, :, :].rearrange("p (r a) q -> p r (a q)", r=RB)
                    hi, lo = (t[:, s, :].rearrange("p (k n) -> p k n", k=4) for t in (w_hi, w_lo))
                    for r in range(RB):
                        for kk in range(4):
                            k = k0 + kk
                            ins = passes(out[:, r, :], tuple(a[:, k, P * r:P * r + P] for a in src),
                                         (hi[:, kk, :], lo[:, kk, :]), first=first and kk == 0, last=last and kk == 3)
                        if last and r == 0:
                            ins.then_inc(row0_full, 1)
                    ins.then_inc(mm_full if last else unit_done, 1)

                def branches(w):
                    s = take_unit(w)
                    hi, lo = (t[:, s, :].rearrange("p (k n) -> p k n", k=8) for t in (w_hi, w_lo))
                    for t in range(2):
                        n = MM_AT[(w, t)]
                        bank = mm_take(n)
                        for br in range(NBR):
                            for c2 in range(2):
                                k = 2 * br + c2
                                sl = slice(P * t, P * t + P)
                                ins = passes(bank[:, br, :], (hi[:, k, sl], lo[:, k, sl]),
                                             (br_hi[:, k, :], br_lo[:, k, :]), first=(c2 == 0), last=(c2 == 1))
                        ins.then_inc(mm_full, 1)

                def forget(src):
                    pe.wait_ge(wf_ready, l + 1)
                    pe.wait_ge(tr_free, l * 2 + 1)
                    for r in range(RB):
                        for k in range(KT):
                            ins = passes(turn[:, 4 * r:4 * r + 4], tuple(a[:, k, P * r:P * r + P] for a in src),
                                         (wf_hi[:, k, :], wf_lo[:, k, :]), first=(k == 0), last=(k == KT - 1))
                    ins.then_inc(tr_full, 1)

                def scores(i):
                    b, h = HEADS[i]
                    st = {"B": 0, "D": 1, "A": 0, "C": 1}[b]
                    if b == "D" and h == 0:
                        pe.wait_ge(masks_in, 16)
                        pe.wait_ge(lf_ready, l + 1)
                    if b in "AC" and h == 0:
                        for j in range(2):
                            k = S_AT[("qk", b, j)]
                            pe.wait_ge(s_free[k % 2], l * (NSMALL // 2) + (PRE_SMALL // 2 + k // 2 + 2))
                    if h == 0 and b in "BD":
                        pe.wait_ge(mm_free[1], l * (NMM // 2) + (1 + (1 if b == "B" else 2)))
                    for j in range(2 if b == "A" else 1):
                        bank = s_take(("s", i, j))
                        dd = 32 if b == "A" else 64
                        hh = 2 * h + j if b == "A" else h
                        per = P // dd
                        p0, ft = dd * (hh % per), hh // per
                        q, k = q_T[st][p0:p0 + dd, ft, :], k_T[st][p0:p0 + dd, ft, :]
                        for blk in range(RB):
                            out = bank[:, P * blk:P * blk + P * (blk + 1)]
                            ins = pe.matmul(out, q[:, P * blk:P * blk + P], k[:, 0:P * (blk + 1)], start=True,
                                            stop=(b != "D"))
                            if b == "D":
                                for jt in range(blk + 1):
                                    ins = pe.matmul(out, lf_b[:, 4 * jt + h, :],
                                                    tab[:, C_NU + SEQ * jt:C_NU + SEQ * jt + P * (blk + 1)],
                                                    start=False, stop=(jt == blk))
                        ins.then_inc(s_full, 1)

                def turn_probs(i):
                    b, h = HEADS[i]
                    if b == "A":
                        pe.wait_ge(mix_ready, l * 4 + (h + 1))
                    else:
                        count = sum({"B": 1, "D": 2, "A": 4, "C": 2}[HEADS[n][0]] for n in range(i + 1))
                        pe.wait_ge(exp_ready, l * 36 + count)
                    if i == 0:
                        pe.wait_ge(tr_free, l * 2 + 2)
                    else:
                        pe.wait_ge(pt_ready, l * 16 + (ONE + i))
                    pr = probs[:, prob_slot(i, 0), :]
                    for t in range(3):
                        ins = pe.transpose(turn[:, P * t:P * t + P], pr[:, P * t:P * t + P], idn)
                    ins.then_inc(tr_full, 1)

                def weigh(i):
                    b, h = HEADS[i]
                    o = i // 4
                    pe.wait_ge(pt_ready, l * 16 + (ONE + i + 1))
                    if h == 0:
                        pe.wait_ge(ov_free, l * 4 + (o + 1))
                    pt, v = p_T[:, i % 2, :], v_of[b]
                    cols = slice(HD * h, HD * h + HD)
                    out0, out1 = ov[:, HD * h:HD * h + HD], ov[:, BW + HD * h:BW + HD * h + HD]
                    pe.matmul(out0, pt[:, 0:P], v[:, 0, cols], start=True, stop=True)
                    pe.matmul(out1, pt[:, P:2 * P], v[:, 0, cols], start=True, stop=False)
                    pe.matmul(out1, pt[:, 2 * P:3 * P], v[:, 1, cols], start=False, stop=True).then_inc(pv_done, 1)
                    if h == 3:
                        pe.wait_ge(pv_done, l * 16 + (i + 1))
                        pe.sem_inc(ov_full, 1)

                def turn_qk(b, j):
                    pe.wait_ge(rope_ready, l * 2 + (1 if b == "A" else 2))
                    bank = s_take(("qk", b, j))
                    for ft in range(2):
                        for r in range(RB):
                            ins = pe.transpose(bank[:, SEQ * ft + P * r:SEQ * ft + P * r + P],
                                               qk_rows[:, r, j, P * ft:P * ft + P], idn)
                    ins.then_inc(s_full, 1)

                def turn_o(o):
                    pe.wait_ge(o_ready, l * 4 + (o + 1))
                    bank = s_take(("o", o, 0))
                    flat = o_rows[:, :, :, :].rearrange("p r h d -> p r (h d)")
                    for c2 in range(2):
                        for r in range(RB):
                            ins = pe.transpose(bank[:, SEQ * c2 + P * r:SEQ * c2 + P * r + P],
                                               flat[:, r, P * c2:P * c2 + P], idn)
                    ins.then_inc(s_full, 1)

                def ada_sum(blk):
                    pe.wait_ge(acc_ready, l * 12 + (PRE_BLOCKS + blk + 1))
                    bank = s_take(("ada", blk, 0))
                    if blk // 2 in GATE_CHUNKS:
                        pe.matmul(bank[:, :], ones[:, 0:P], acc[:, blk % 2, :], start=True, stop=True)\
                            .then_inc(s_full, 1)
                    else:
                        ada_columns(bank, blk % 2)

                h = (h_hi, h_lo)
                turn_x(0)
                pe.wait_ge(cv_in, l * 32 + 32)
                pe.wait_ge(pt_ready, l * 16 + ONE)
                pe.transpose(turn[:, 0:P], cv_rows[:, :], idn).then_inc(tr_full, 1)

                for u in range(UNITS):
                    if u < U_BR:
                        form = IN_BLOCKS[u // 2][1] if u < U_GATE else "TT"
                        if u < 2:
                            pe.wait_ge(h_hi_ready, l * 8 + 2 * (u + 1))
                            pe.wait_ge(h_lo_ready, l * 8 + 2 * (u + 1))
                        features_or_rows(u, MM_AT[(u | 1, 0)], form, h, u % 2)
                    elif u < U_O:
                        if u == U_BR:
                            pe.wait_ge(br_hi_ready, l * 4 + 4)
                            pe.wait_ge(br_lo_ready, l * 4 + 4)
                        branches(u)
                    elif u < U_UP:
                        ob, kb = O_ORDER[u - U_O]
                        if ob == 0:
                            pe.wait_ge(m_hi_ready, l * KT + 4 * (kb + 1))
                            pe.wait_ge(m_lo_ready, l * KT + 4 * (kb + 1))
                        rows(u, MM_AT[(U_O + 2 + ob, 0)], h, 4 * kb, kb == 0, kb == 1)
                    elif u < U_DOWN:
                        if u == U_UP:
                            turn_x(1)
                        if u < U_UP + 2:
                            pe.wait_ge(h_hi_ready, l * 8 + 4 + 2 * (u - U_UP + 1))
                            pe.wait_ge(h_lo_ready, l * 8 + 4 + 2 * (u - U_UP + 1))
                        features_or_rows(u, MM_AT[(u | 1, 0)], "TT", h, u % 2)
                    else:
                        ob, kb = DOWN_ORDER[u - U_DOWN]
                        if ob == 0:
                            pe.wait_ge(act_hi_ready, l * 4 + (kb + 1))
                            pe.wait_ge(act_lo_ready, l * 4 + (kb + 1))
                        rows(u, MM_AT[(U_DOWN + 6 + ob, 0)], (act_hi, act_lo), 4 * kb, kb == 0, kb == 3)
                    if u == 1:
                        forget(h)
                    if score_head(u) is not None:
                        scores(score_head(u))
                    if 0 <= u - 8 < 16:
                        turn_probs(u - 8)
                    if 0 <= u - 9 < 16:
                        weigh(u - 9)
                    if u in QK_AFTER:
                        turn_qk(*QK_AFTER[u])
                    if u in OT_AFTER:
                        turn_o(OT_AFTER[u])
                    if u in ADA_AFTER:
                        ada_sum(ADA_AFTER[u])


_INS = ["x", "c", "positions", "w_ada", "b_ada", "w_in", "lam_q1", "lam_k1", "lam_q2", "lam_k2", "subln_g", "forget_b",
        "w_branch", "w_o", "ln1_g", "ln1_b", "w_up", "conv_w", "conv_b", "w_down", "ln2_g", "ln2_b"]


def kernel(**inputs):
    import numpy as _np
    import concourse.bacc as _bacc
    from concourse import mybir as _mybir
    from concourse.bass_utils import run_bass_kernel_spmd as _run

    nc = _bacc.Bacc("TRN2", target_bir_lowering=False, num_devices=1)
    arrays, args = {}, []
    for name in _INS:
        a = _np.ascontiguousarray(inputs[name])
        arrays[f"in_{name}_dram"] = a
        args.append(nc.dram_tensor(f"in_{name}_dram", a.shape, _mybir.dt.from_np(a.dtype), kind="ExternalInput").ap())
    t = constants()
    arrays["table_dram"] = t
    args.append(nc.dram_tensor("table_dram", t.shape, _mybir.dt.float32, kind="ExternalInput").ap())
    o = nc.dram_tensor("out_0_dram", (1, SEQ, D), _mybir.dt.float32, kind="ExternalOutput").ap()
    build(nc, *args, o)
    return _run(nc, [arrays], core_ids=[0]).results[0]["out_0_dram"]
```
